# Optimizing a Trainium2 kernel written in Bass

```python
import math
import jax, jax.numpy as jnp
from jax import lax
import numpy as np

D_MODEL = 2048
BATCH = 1
SEQ = 512
DEPTH = 1

CHUNK = 64
Q_BLOCK = 128
N_ATTN_HEADS = 8
ATTN_HEAD_DIM = 64
ATTN_V_DIM = 2 * ATTN_HEAD_DIM
ATTN_WIDTH = N_ATTN_HEADS * ATTN_V_DIM
CONV_WIDTH = D_MODEL - ATTN_WIDTH
CONV_GROUPS = 8
CONV_K = 3
D_FF = (8 * D_MODEL + 3 * 256 - 1) // (3 * 256) * 256
ROPE_THETA = 10000.0
EPS = 1e-6
SUBLN_EPS = 1e-5
QK_COLS = N_ATTN_HEADS * 2 * ATTN_HEAD_DIM
IN_COLS = 2 * QK_COLS + ATTN_WIDTH + 3 * CONV_WIDTH

kernel_name = "hybrid_diffattn_shortconv_block"

def lambda_init(layer_idx):
    return 0.8 - 0.6 * math.exp(-0.3 * layer_idx)

def rms_norm(x, w, eps=EPS):
    xf = x.astype(jnp.float32)
    y = xf * lax.rsqrt(jnp.mean(xf * xf, axis=-1, keepdims=True) + eps)
    return (y * w.astype(jnp.float32)).astype(x.dtype)

def rope(t, cos, sin):
    tf = t.astype(jnp.float32)
    half = tf.shape[-1] // 2
    t1, t2 = tf[..., :half], tf[..., half:]
    c = cos[None, :, None, None, :]
    s = sin[None, :, None, None, :]
    out = jnp.concatenate([t1 * c - t2 * s, t2 * c + t1 * s], axis=-1)
    return out.astype(t.dtype)

def diff_attention(q, k, v, lam):
    b, s, h, _, dk = q.shape
    nb = s // Q_BLOCK
    scale = 1.0 / math.sqrt(dk)
    qb = q.reshape(b, nb, Q_BLOCK, h, 2, dk).transpose(1, 0, 2, 3, 4, 5)
    key_chunk = jnp.arange(s) // CHUNK

    def block(args):
        qi, i = args
        q_chunk = (i * Q_BLOCK + jnp.arange(Q_BLOCK)) // CHUNK
        mask = key_chunk[None, :] <= q_chunk[:, None]
        sc = jnp.einsum('bqhcd,bkhcd->bhcqk', qi, k).astype(jnp.float32) * scale
        sc = jnp.where(mask[None, None, None], sc, -1e30)
        p = jax.nn.softmax(sc, axis=-1)
        a = p[:, :, 0] - lam * p[:, :, 1]
        return jnp.einsum('bhqk,bkhd->bqhd', a.astype(v.dtype), v)

    out = lax.map(block, (qb, jnp.arange(nb)))
    return out.transpose(1, 0, 2, 3, 4).reshape(b, s, h, v.shape[-1])

def causal_depthwise_conv(u, w):
    c = u.shape[-1]
    return lax.conv_general_dilated(
        u, w[:, None, :].astype(u.dtype), window_strides=(1,),
        padding=[(CONV_K - 1, 0)], dimension_numbers=('NWC', 'WIO', 'NWC'),
        feature_group_count=c)

def setup_inputs(seed: int = 0) -> dict:
    key = jax.random.key(seed)
    ks = jax.random.split(key, 16)
    f32 = jnp.float32
    nrm = lambda k, shape, s: jax.random.normal(k, shape, f32) * s
    return {
        "x": jax.random.normal(ks[0], (BATCH, SEQ, D_MODEL), f32),
        "attn_norm_w": 1.0 + nrm(ks[1], (DEPTH, D_MODEL), 0.02),
        "w_in": nrm(ks[2], (DEPTH, D_MODEL, IN_COLS), D_MODEL ** -0.5),
        "q_norm_w": 1.0 + nrm(ks[3], (DEPTH, ATTN_HEAD_DIM), 0.02),
        "k_norm_w": 1.0 + nrm(ks[4], (DEPTH, ATTN_HEAD_DIM), 0.02),
        "lambda_q1": nrm(ks[5], (DEPTH, ATTN_HEAD_DIM), 0.1),
        "lambda_k1": nrm(ks[6], (DEPTH, ATTN_HEAD_DIM), 0.1),
        "lambda_q2": nrm(ks[7], (DEPTH, ATTN_HEAD_DIM), 0.1),
        "lambda_k2": nrm(ks[8], (DEPTH, ATTN_HEAD_DIM), 0.1),
        "subln_w": 1.0 + nrm(ks[9], (DEPTH, ATTN_V_DIM), 0.02),
        "conv_w": nrm(ks[10], (DEPTH, CONV_K, CONV_WIDTH), CONV_K ** -0.5),
        "w_out": nrm(ks[11], (DEPTH, D_MODEL, D_MODEL), D_MODEL ** -0.5),
        "ffn_norm_w": 1.0 + nrm(ks[12], (DEPTH, D_MODEL), 0.02),
        "w_gate": nrm(ks[13], (DEPTH, D_MODEL, D_FF), D_MODEL ** -0.5),
        "w_up": nrm(ks[14], (DEPTH, D_MODEL, D_FF), D_MODEL ** -0.5),
        "w_down": nrm(ks[15], (DEPTH, D_FF, D_MODEL), D_FF ** -0.5),
    }

def reference(x, attn_norm_w, w_in, q_norm_w, k_norm_w, lambda_q1, lambda_k1,
              lambda_q2, lambda_k2, subln_w, conv_w, w_out, ffn_norm_w,
              w_gate, w_up, w_down):
    b, s, _ = x.shape
    pos = jnp.arange(s, dtype=jnp.float32)
    inv_freq = ROPE_THETA ** (-jnp.arange(0, ATTN_HEAD_DIM, 2, dtype=jnp.float32) / ATTN_HEAD_DIM)
    ang = pos[:, None] * inv_freq[None, :]
    cos, sin = jnp.cos(ang), jnp.sin(ang)

    h_res = x
    for l in range(DEPTH):
        lam_init = lambda_init(l)
        xn = rms_norm(h_res, attn_norm_w[l])
        proj = jnp.einsum('bsd,de->bse', xn, w_in[l])
        o1 = QK_COLS
        o2 = o1 + QK_COLS
        o3 = o2 + ATTN_WIDTH
        o4 = o3 + CONV_WIDTH
        o5 = o4 + CONV_WIDTH
        q = proj[..., :o1].reshape(b, s, N_ATTN_HEADS, 2, ATTN_HEAD_DIM)
        k = proj[..., o1:o2].reshape(b, s, N_ATTN_HEADS, 2, ATTN_HEAD_DIM)
        v = proj[..., o2:o3].reshape(b, s, N_ATTN_HEADS, ATTN_V_DIM)
        gate_b = proj[..., o3:o4]
        gate_c = proj[..., o4:o5]
        hc = proj[..., o5:]

        q = rope(rms_norm(q, q_norm_w[l]), cos, sin)
        k = rope(rms_norm(k, k_norm_w[l]), cos, sin)
        lam = (jnp.exp(jnp.sum(lambda_q1[l].astype(jnp.float32) * lambda_k1[l].astype(jnp.float32)))
               - jnp.exp(jnp.sum(lambda_q2[l].astype(jnp.float32) * lambda_k2[l].astype(jnp.float32)))
               + lam_init)
        attn = diff_attention(q, k, v, lam)
        attn = rms_norm(attn, subln_w[l], SUBLN_EPS) * (1.0 - lam_init)
        attn = attn.reshape(b, s, ATTN_WIDTH)

        conv = gate_b * causal_depthwise_conv(gate_c * hc, conv_w[l])

        mixed = jnp.concatenate([attn.astype(conv.dtype), conv], axis=-1)
        h_res = h_res + jnp.einsum('bse,ed->bsd', mixed, w_out[l])

        fn = rms_norm(h_res, ffn_norm_w[l])
        g = jnp.einsum('bsd,df->bsf', fn, w_gate[l])
        u = jnp.einsum('bsd,df->bsf', fn, w_up[l])
        h_res = h_res + jnp.einsum('bsf,fd->bsd', jax.nn.silu(g) * u, w_down[l])
    return h_res


_drawn_inputs = setup_inputs


def setup_inputs(seed=0):
    import zlib

    import numpy as np

    out = dict(_drawn_inputs(seed))
    spreads = {}
    factors = {'q_norm_w': 4.83,
     'k_norm_w': 6.155,
     'lambda_q1': 8.0,
     'lambda_k2': 3.214,
     'subln_w': 5.561,
     'ffn_norm_w': 4.991}
    for name, (base, spread) in spreads.items():
        noise = np.random.default_rng([zlib.crc32(name.encode()), seed]).standard_normal(out[name].shape)
        drawn = base * np.exp(spread * noise) if base else spread * noise
        out[name] = __import__('jax').numpy.asarray(drawn.astype(out[name].dtype))
    for name, factor in factors.items():
        out[name] = (out[name] * factor).astype(out[name].dtype)
    return out
```

```python
import numpy as np
import concourse.bass as bass
from concourse import mybir

F32, F32R = mybir.dt.float32, mybir.dt.float32r
ALU = mybir.AluOpType
ACT = mybir.ActivationFunctionType
AX = mybir.AxisListType

P = 128
D = 2048
SEQ = 512
HEADS = 8
DK = 64
DV = 128
FF = 5632
CHUNK = 64
CONV_K = 3
EPS = 1e-6
SUBLN_EPS = 1e-5
LAMBDA_INIT = 0.8 - 0.6 * float(np.exp(0.0))
ROPE_THETA = 10000.0
SCALE = DK ** -0.5
MASKED = -1e30

ST = SEQ // P
KT = D // P
NB = 512
UK = 4
UNIT = UK * NB
QKV_BLOCKS = 3 * HEADS * DV // NB
OUT_BLOCKS = D // NB
CONV_COLS = 3 * HEADS * DV
FT = FF // P
CHUNKS = 4
CF = FT // CHUNKS
DOWN_UNITS = (4, 4, 3)
assert sum(DOWN_UNITS) == CF

U_QKV = 0
U_HEAD = U_QKV + QKV_BLOCKS * KT // UK
U_OUT = U_HEAD + 3 * HEADS
U_FF = U_OUT + OUT_BLOCKS * KT // UK
U_CHUNK = 2 * CF + OUT_BLOCKS * len(DOWN_UNITS)

E_QKV = ST * KT // 4
E_HEAD = E_QKV + ST * QKV_BLOCKS
E_OUT = E_HEAD + 2 * HEADS
E_NORM2 = E_OUT + ST * OUT_BLOCKS
E_FF = E_NORM2 + ST * KT // 4
E_CHUNK = CF + ST * OUT_BLOCKS

T_OUT = (ST - 1) * QKV_BLOCKS
T_FF = T_OUT + (ST - 1) * OUT_BLOCKS
T_CHUNK = (ST - 1) * OUT_BLOCKS

PREP = 8
CONSTS = 9

E_END = E_FF + CHUNKS * E_CHUNK

SLOTS = 24
SCORES_AT = {0: 0, 4: 1, 8: 2, 12: 3}
TURN_AT = {5: 0, 9: 1, 13: 2, 17: 3}
VALUES_AT = {6: 0, 10: 1, 14: 2, 18: 3}
PLACE_AT = {9: 0, 13: 1, 17: 2, 21: 3}
QK_TURN_AT = {20: 0, 22: 1}

BASE = 1152


def rope_tables():
    freq = (ROPE_THETA ** (-np.arange(0, DK, 2, dtype=np.float32) / np.float32(DK))).astype(np.float32)
    angle = np.arange(SEQ, dtype=np.float32)[:, None] * freq[None, :]
    both = np.stack([np.cos(angle), np.sin(angle)]).astype(np.float32)
    return np.ascontiguousarray(both.reshape(2, ST, P, DK // 2).transpose(2, 0, 1, 3))


def build(nc, x, attn_norm_w, w_in, q_norm_w, k_norm_w, lambda_q1, lambda_k1, lambda_q2, lambda_k2,
          subln_w, conv_w, w_out, ffn_norm_w, w_gate, w_up, w_down, rope_cs, out):
    K = 1024
    cursor = [BASE]

    def region(size):
        start = cursor[0]
        cursor[0] += size
        return start

    def at(name, offset, shape, dt=F32):
        return nc.alloc_sbuf_tensor_at(name, shape, dt, offset=offset)

    act_hi = at("act_hi", region(32 * K), [P, KT, SEQ], F32R)
    act_lo = at("act_lo", region(32 * K), [P, KT, SEQ], F32R)
    w_raw = at("w_raw", region(16 * K), [P, 2, UNIT])
    w_hi = at("w_hi", region(16 * K), [P, 2, UNIT], F32R)
    w_lo = at("w_lo", region(16 * K), [P, 2, UNIT], F32R)
    wide = region(48 * K)
    qkv = at("qkv", wide, [P, ST, 3 * HEADS * DV])
    norm_w = at("norm_w", wide, [P, D])
    scaled = at("scaled", wide + 8 * K, [P, 2, D])
    squares = at("squares", wide + 24 * K, [P, D])
    hid_hi = at("hid_hi", wide, [P, CF, SEQ], F32R)
    hid_lo = at("hid_lo", wide + 2 * CF * K, [P, CF, SEQ], F32R)
    tall = region(32 * K)
    x_nat = at("x_nat", tall, [P, ST, D])
    mixed = at("mixed", tall, [P, KT, SEQ])
    resid = at("resid", tall, [P, ST, D])
    work = region(24 * K)
    expo = at("expo", work, [P, 2, 2, NB])
    probs_t = at("probs_t", work + 8 * K, [P, NB])
    q_t = at("q_t", work + 10 * K, [P, SEQ])
    k_t = at("k_t", work + 12 * K, [P, SEQ])
    rot = at("rot", work + 14 * K, [P, 2, ST, DV])
    rot_tmp = at("rot_tmp", work + 18 * K, [P, ST, DV])
    gated = at("gated", work + 20 * K, [P, SEQ + CONV_K])
    attn_n = at("attn_n", work + 23 * K, [P, DV])
    silu_g = at("silu_g", work, [P, SEQ])
    hidden = at("hidden", work + 2 * K, [P, SEQ])
    small = region(4 * K)
    at_small = [small]

    def col(name, shape):
        n = 4 * int(np.prod(shape[1:]))
        t = at(name, at_small[0], shape)
        at_small[0] += -(-n // 32) * 32
        assert at_small[0] <= small + 4 * K
        return t

    ident = col("ident", [P, P])
    cs = col("cs", [P, 2, ST, DK // 2])
    qk_w = col("qk_w", [P, 2, DK])
    lam_in = col("lam_in", [P, 4, DK])
    rows = at("rows", work, [CONV_K * HEADS + 1, P])
    taps = col("taps", [P, CONV_K * HEADS + 1])
    lam_sum = col("lam_sum", [P, 2])
    lam_exp = col("lam_exp", [P, 2])
    neg_lam = col("neg_lam", [P, 2])
    half_power = col("half_power", [P, 8])
    x_ssq = col("x_ssq", [P, ST])
    x_rstd = col("x_rstd", [P, 2, ST])
    r_part = col("r_part", [P, ST, OUT_BLOCKS])
    r_ssq = col("r_ssq", [P, ST])
    qk_ssq = col("qk_ssq", [P, 2 * ST])
    qk_ms = col("qk_ms", [P, 2 * ST])
    qk_rstd = col("qk_rstd", [P, 2 * ST])
    peak = col("peak", [P, 2, 2])
    neg_peak = col("neg_peak", [P, 2, 2])
    total = col("total", [P, 2, 2])
    share = col("share", [P, 2, 2])
    o_ssq = col("o_ssq", [P, 2])
    o_ms = col("o_ms", [P, 2])
    o_rstd = col("o_rstd", [P, 2])
    assert cursor[0] <= nc.sbuf_usable_end

    bank = nc.alloc_psum_tensor("bank", [P, 8, NB], F32)
    SCORE_BANK = (2, 4)
    TURN_BANK, VALUE_BANK = 6, 7
    CONV_BANK = (0, 1, 0)
    BLOCK_BANKS = ((0, 1, 2, 3), (4, 5, 6, 7))
    NORM_BANKS = (4, 0)
    DOWN_BANKS = ((2, 3, 0, 1), (4, 5, 6, 7))

    sem = nc.alloc_semaphore
    s_consts = sem("consts_loaded")
    s_norm_w = sem("norm_w_loaded")
    s_x = [sem(f"x_loaded{t}") for t in range(ST)]
    s_resid = sem("resid_loaded")
    s_norm_w2 = sem("norm_w2_loaded")
    s_raw = [sem(f"w_raw_loaded{p}") for p in range(2)]
    s_out = sem("out_written")
    s_ident = sem("ident_made")
    s_half = sem("half_power_made")
    s_ssq = sem("row_ssq_made")
    s_rsum = sem("resid_ssq_made")
    s_rstd = sem("row_rstd_steps")
    s_scaled = sem("row_scaled")
    s_turned = sem("act_turned")
    s_act_hi = sem("act_hi_made")
    s_rows_t = sem("rows_turned")
    s_taps = sem("taps_made")
    s_lam = sem("lambda_steps")
    s_lam_exp = sem("lambda_exp")
    s_whi = sem("w_hi_made")
    s_wlo = sem("w_lo_made")
    s_used = sem("w_used")
    s_tile = sem("tile_sum")
    s_emptied = sem("emptied")
    s_act_out = sem("act_emptied")
    s_prep = sem("prep_steps")
    s_prep_ms = sem("prep_mean_square")
    s_qk_in = sem("qk_copied")
    s_qk_turn = sem("qk_turned")
    s_qk_t = sem("qk_t_ready")
    s_scores = sem("scores_ready")
    s_mask = sem("scores_masked")
    s_peak = sem("peak_found")
    s_neg = sem("neg_peak_made")
    s_exp = sem("exp_made")
    s_share = sem("share_steps")
    s_probs = sem("probs_ready")
    s_pturn = sem("probs_turned")
    s_probs_t = sem("probs_t_ready")
    s_values = sem("values_summed")
    s_ossq = sem("attn_mean_square")
    s_orstd = sem("attn_rstd")
    s_attn_n = sem("attn_normed")
    s_oturn = sem("attn_turned")
    s_placed = sem("attn_placed")
    s_pad = sem("conv_pad")
    s_conv = sem("conv_steps")
    s_mix_hi = sem("mixed_hi_made")
    s_low = sem("operand_lo_made")
    s_hid_hi = sem("hidden_hi_made")

    w_in_v = w_in[0].rearrange("(k p) n -> p k n", p=P)
    w_out_v = w_out[0].rearrange("(k p) n -> p k n", p=P)
    w_gate_v = w_gate[0].rearrange("(k p) n -> p k n", p=P)
    w_up_v = w_up[0].rearrange("(k p) n -> p k n", p=P)
    w_down_v = w_down[0].rearrange("(k p) n -> p k n", p=P)
    x_v = x[0].rearrange("(t p) d -> p t d", p=P)
    out_v = out[0].rearrange("(t p) d -> p t d", p=P)

    def moving(w, slot):
        return w[:, slot, :].rearrange("p (k n) -> p k n", n=NB)

    def stationary(w, slot):
        return w[:, slot, :].rearrange("p (k n) -> p k n", n=P)

    block = nc.Block()
    with block:

        @block.sync
        def _(sp):
            def load(half, parity, source, first=False):
                rows_, columns = source.shape[1], source.shape[2]
                if not first:
                    sp.wait_ge(s_wlo, 2 * half + parity - 1)
                dst = w_raw[:, parity, 0:rows_ * columns].rearrange("p (k n) -> p k n", n=columns)
                sp.dma_start(dst, source).then_inc(s_raw[parity], 16)

            def qkv_source(blk, m):
                return w_in_v[:, UK * m:UK * m + UK, bass.ds(blk * NB, NB)]

            sp.dma_start(x_nat[:, 0, :], x_v[:, 0, :]).then_inc(s_x[0], 16)
            load(0, 0, qkv_source(0, 0), first=True)
            sp.dma_start(x_nat[:, 1, :], x_v[:, 1, :]).then_inc(s_x[1], 16)
            load(0, 1, qkv_source(0, 1), first=True)
            sp.dma_start(x_nat[:, 2, :], x_v[:, 2, :]).then_inc(s_x[2], 16)
            sp.dma_start(x_nat[:, 3, :], x_v[:, 3, :]).then_inc(s_x[3], 16)
            load(1, 0, qkv_source(0, 2))
            load(1, 1, qkv_source(0, 3))
            with sp.Fori(1, QKV_BLOCKS) as blk:
                for m in range(4):
                    load(blk * 2 + m // 2, m % 2, qkv_source(blk, m))
            with sp.Fori(0, HEADS // 2) as pair:
                for m in range(6):
                    sub, part = divmod(m, 3)
                    column = CONV_COLS + (1, 2, 0)[part] * HEADS * DV + sub * DV
                    load(pair * 3 + U_HEAD // 2 + m // 2, m % 2,
                         w_in_v[:, :, bass.ds(pair * (2 * DV) + column, DV)])
            with sp.Fori(0, OUT_BLOCKS) as blk:
                for m in range(4):
                    load(blk * 2 + U_OUT // 2 + m // 2, m % 2,
                         w_out_v[:, UK * m:UK * m + UK, bass.ds(blk * NB, NB)])
            with sp.Fori(0, CHUNKS) as c:
                with sp.Fori(0, CF) as j:
                    unit = c * (U_CHUNK // 2) + j + U_FF // 2
                    column = c * (CF * P) + j * P
                    load(unit, 0, w_gate_v[:, :, bass.ds(column, P)])
                    load(unit, 1, w_up_v[:, :, bass.ds(column, P)])
                with sp.Fori(0, OUT_BLOCKS // 2) as d:
                    for m in range(6):
                        sub, part = divmod(m, 3)
                        load(c * (U_CHUNK // 2) + d * 3 + U_FF // 2 + CF + m // 2, m % 2,
                             w_down_v[:, bass.ds(c * CF + 4 * part, DOWN_UNITS[part]),
                                      bass.ds(d * (2 * NB) + sub * NB, NB)])
            with sp.Fori(0, OUT_BLOCKS) as d:
                for t in range(ST):
                    sp.wait_ge(s_emptied, d * ST + E_END - ST * OUT_BLOCKS + t + 1)
                    sp.dma_start(out_v[:, t, bass.ds(d * NB, NB)],
                                 resid[:, t, bass.ds(d * NB, NB)]).then_inc(s_out, 16)
            sp.wait_ge(s_out, 16 * ST * OUT_BLOCKS)

        @block.gpsimd
        def _(pool):
            pool.memset(ident[:, :], 0.0).then_inc(s_ident, 1)
            pool.memset(half_power[:, :], -0.5).then_inc(s_half, 1)
            pool.wait_ge(s_ident, 1)
            pool.affine_select(out=ident[:, :], in_=ident[:, :], compare_op=ALU.not_equal, fill=1.0, base=0,
                               pattern=[[-1, P]], channel_multiplier=1).then_inc(s_ident, 1)
            pool.wait_ge(s_half, 1)

            def row_rstd(phase, t):
                r, n = x_rstd[:, phase, t:t + 1], 2 * (ST * phase + t)
                if phase == 0:
                    pool.wait_ge(s_ssq, t + 1)
                else:
                    pool.wait_ge(s_rsum, t + 1)
                ssq = (x_ssq, r_ssq)[phase][:, t:t + 1]
                pool.tensor_scalar(r, ssq, 1.0 / D, EPS, ALU.mult, ALU.add).then_inc(s_rstd, 1)
                pool.wait_ge(s_rstd, n + 1)
                pool.tensor_tensor(r, r, half_power[:, 0:1], ALU.pow).then_inc(s_rstd, 1)

            def prep_step(head, part, step):
                new, tmp = rot[:, part, :, :], rot_tmp[:, :, :]
                halves, tmp_halves = (a.rearrange("p t (c e) -> p (t c) e", c=2) for a in (new, tmp))
                quarters, tmp_quarters = (a.rearrange("p t (c e) -> p t c e", c=4) for a in (new, tmp))
                shape, h = [P, ST, 4, DK // 2], DK // 2
                pool.wait_ge(s_prep, head * (2 * PREP) + part * PREP + step + 1)
                if step == 0:
                    pool.wait_ge(s_qk_in, head * 2 + part + 1)
                    ins = pool.tensor_tensor(tmp, new, new, ALU.mult)
                elif step == 1:
                    pool.wait_ge(s_prep_ms, head * 4 + 2 * part + 2)
                    ins = pool.tensor_tensor(qk_rstd[:, :], qk_ms[:, :], half_power[:, :], ALU.pow)
                elif step == 2:
                    rstd = qk_rstd[:, :].rearrange("p (t c) -> p t c", c=2).unsqueeze(3).to_broadcast([P, ST, 2, DK])
                    both = new.rearrange("p t (c e) -> p t c e", c=2)
                    ins = pool.tensor_tensor(both, both, rstd, ALU.mult)
                elif step == 3:
                    weight = qk_w[:, part, :].unsqueeze(1).to_broadcast([P, 2 * ST, DK])
                    ins = pool.tensor_tensor(halves, halves, weight, ALU.mult)
                elif step == 4:
                    ins = pool.tensor_tensor(tmp_quarters, quarters, cs[:, 1, :, :].unsqueeze(2).to_broadcast(shape), ALU.mult)
                elif step == 5:
                    ins = pool.tensor_tensor(quarters, quarters, cs[:, 0, :, :].unsqueeze(2).to_broadcast(shape), ALU.mult)
                elif step == 6:
                    ins = pool.tensor_tensor(halves[:, :, 0:h], halves[:, :, 0:h], tmp_halves[:, :, h:DK], ALU.subtract)
                else:
                    ins = pool.tensor_tensor(halves[:, :, h:DK], halves[:, :, h:DK], tmp_halves[:, :, 0:h], ALU.add)
                ins.then_inc(s_prep, 1)

            def attn_rstd(head, i):
                e = slice(i % 2, i % 2 + 1)
                pool.wait_ge(s_ossq, head * 8 + 2 * i + 2)
                pool.tensor_tensor(o_rstd[:, e], o_ms[:, e], half_power[:, 0:1], ALU.pow).then_inc(s_orstd, 1)

            def pool_head(head, last=False):
                for s in range(SLOTS):
                    if s < 2 * PREP and not last:
                        prep_step(head + 1, s // PREP, s % PREP)
                    if s - 1 in VALUES_AT:
                        attn_rstd(head, VALUES_AT[s - 1])

            for t in range(ST):
                row_rstd(0, t)
            pool.wait_ge(s_consts, 16 * CONSTS)
            pool.memset(qk_rstd[:, :], 0.0).then_inc(s_prep, 1)
            for part in range(2):
                for step in range(PREP):
                    prep_step(0, part, step)
            with pool.Fori(0, HEADS // 2 - 1) as pair:
                pool_head(pair * 2)
                pool_head(pair * 2 + 1)
            pool_head(HEADS - 2)
            pool_head(HEADS - 1, last=True)
            for t in range(ST):
                row_rstd(1, t)

        @block.scalar
        def _(act):
            act.dma_start(norm_w[:, :], attn_norm_w[0, :].partition_broadcast(P)).then_inc(s_norm_w, 16)
            taps_rows = CONV_K * HEADS
            act.dma_start(rows[0:taps_rows, :], conv_w[0].rearrange("j (h p) -> (j h) p", p=P)).then_inc(s_consts, 16)
            act.dma_start(rows[taps_rows:taps_rows + 1, :], subln_w).then_inc(s_consts, 16)
            act.dma_start(cs[:, :, :, :], rope_cs).then_inc(s_consts, 16)
            for n, w in enumerate((q_norm_w, k_norm_w)):
                act.dma_start(qk_w[:, n, :], w[0, :].partition_broadcast(P)).then_inc(s_consts, 16)
            for n, w in enumerate((lambda_q1, lambda_k1, lambda_q2, lambda_k2)):
                act.dma_start(lam_in[:, n, :], w[0, :].partition_broadcast(P)).then_inc(s_consts, 16)

            def round_unit(half, parity, size=UNIT, first=False):
                act.wait_ge(s_raw[parity], half * 16 + 16)
                if not first:
                    act.wait_ge(s_used, half * 2 + parity - 1)
                act.activation(w_hi[:, parity, 0:size], w_raw[:, parity, 0:size], ACT.Copy).then_inc(s_whi, 1)

            def turned_hi(phase, t):
                for b in range(4):
                    act.wait_ge(s_turned, 4 * (ST * phase + t) + b + 1)
                    src = bank[:, NORM_BANKS[phase] + b, :].rearrange("p (k s) -> p k s", s=P)
                    act.activation(act_hi[:, 4 * b:4 * b + 4, t * P:(t + 1) * P], src, ACT.Copy).then_inc(s_act_hi, 1)

            def x_square(t):
                act.wait_ge(s_x[t], 16)
                if t > 0:
                    act.wait_ge(s_ssq, t)
                act.activation(squares[:, :], x_nat[:, t, :], ACT.Square, accum_out=x_ssq[:, t:t + 1]).then_inc(s_ssq, 1)

            x_square(0)
            x_square(1)
            for t in range(ST):
                turned_hi(0, t)
                if t + 2 < ST:
                    x_square(t + 2)
                if t < 2:
                    round_unit(0, t, first=True)
            act.wait_ge(s_lam, 2)
            act.activation(lam_exp[:, :], lam_sum[:, :], ACT.Exp).then_inc(s_lam_exp, 1)

            with act.Fori(0, QKV_BLOCKS // 2) as pair:
                for m in range(8):
                    round_unit(pair * 4 + U_QKV // 2 + 1 + m // 2, m % 2)

            def scores_exp(head, i):
                e = i % 2
                act.wait_ge(s_neg, head * 4 + i + 1)
                for c in range(2):
                    act.activation(expo[:, e, c, 0:(i + 1) * P], bank[:, SCORE_BANK[e] + c, 0:(i + 1) * P], ACT.Exp,
                                   bias=neg_peak[:, e, c:c + 1], scale=SCALE,
                                   accum_out=total[:, e, c:c + 1]).then_inc(s_exp, 1)

            def qk_out(head, part):
                act.wait_ge(s_qk_turn, head * 2 + part + 1)
                act.activation((q_t, k_t)[part][:, :], bank[:, TURN_BANK, :], ACT.Copy).then_inc(s_qk_t, 1)

            def qk_in(head, part):
                act.activation(rot[:, part, :, :], qkv[:, :, bass.ds(head * DV + part * HEADS * DV, DV)],
                               ACT.Copy).then_inc(s_qk_in, 1)

            def act_head(pair, sub, last=False):
                head = pair * 2 + sub
                for s in range(SLOTS):
                    if s % 8 == 0 and s > 0:
                        m = 3 * sub + s // 8 - 1
                        round_unit(pair * 3 + U_HEAD // 2 + 1 + m // 2, m % 2)
                    if s == 8:
                        act.wait_ge(s_used, head * 3 + U_HEAD + 1)
                        act.activation(gated[:, CONV_K - 1:CONV_K - 1 + SEQ], bank[:, CONV_BANK[0], :], ACT.Copy)\
                            .then_inc(s_act_out, 1)
                    if s - 2 in SCORES_AT:
                        scores_exp(head, SCORES_AT[s - 2])
                    if s in TURN_AT:
                        i = TURN_AT[s]
                        act.wait_ge(s_pturn, head * 4 + i + 1)
                        act.activation(probs_t[:, 0:(i + 1) * P], bank[:, TURN_BANK, 0:(i + 1) * P], ACT.Copy)\
                            .then_inc(s_probs_t, 1)
                    if s - 1 in VALUES_AT:
                        i = VALUES_AT[s - 1]
                        act.wait_ge(s_values, head * 4 + i + 1)
                        act.activation(attn_n[:, :], bank[:, VALUE_BANK, 0:DV], ACT.Square,
                                       accum_out=o_ssq[:, i % 2:i % 2 + 1]).then_inc(s_ossq, 1)
                        act.wait_ge(s_ossq, head * 8 + 2 * i + 1)
                        act.activation(o_ms[:, i % 2:i % 2 + 1], o_ssq[:, i % 2:i % 2 + 1], ACT.Copy,
                                       bias=SUBLN_EPS, scale=1.0 / DV).then_inc(s_ossq, 1)
                    if s - 2 in VALUES_AT:
                        i = VALUES_AT[s - 2]
                        act.wait_ge(s_orstd, head * 4 + i + 1)
                        act.activation(attn_n[:, :], bank[:, VALUE_BANK, 0:DV], ACT.Copy,
                                       scale=o_rstd[:, i % 2:i % 2 + 1]).then_inc(s_attn_n, 1)
                    if s in (1, 2) and not last:
                        qk_in(head + 1, s - 1)
                    if s - 1 in QK_TURN_AT and not last:
                        qk_out(head + 1, QK_TURN_AT[s - 1])
                m = 3 * sub + 2
                round_unit(pair * 3 + U_HEAD // 2 + 1 + m // 2, m % 2)

            act.wait_ge(s_emptied, E_QKV + ST * 4)
            for part in range(2):
                qk_in(0, part)
            for part in range(2):
                qk_out(0, part)
            with act.Fori(0, HEADS // 2 - 1) as pair:
                act_head(pair, 0)
                act_head(pair, 1)
            act_head(HEADS // 2 - 1, 0)
            act_head(HEADS // 2 - 1, 1, last=True)

            act.wait_ge(s_used, U_OUT)
            act.dma_start(norm_w[:, :], ffn_norm_w[0, :].partition_broadcast(P)).then_inc(s_norm_w2, 16)
            act.wait_ge(s_placed, 4 * HEADS)
            for k in range(KT):
                if k >= HEADS:
                    act.wait_ge(s_emptied, E_HEAD + 2 * (k - HEADS) + 2)
                act.activation(act_hi[:, k, :], mixed[:, k, :], ACT.Copy).then_inc(s_mix_hi, 1)
            act.wait_ge(s_low, KT)
            act.dma_start(resid[:, :, :], x_v).then_inc(s_resid, 16)

            with act.Fori(0, OUT_BLOCKS // 2) as pair:
                for m in range(8):
                    round_unit(pair * 4 + U_OUT // 2 + 1 + m // 2, m % 2)
                    if m % 4 == 3:
                        for t in range(ST):
                            act.wait_ge(s_emptied, pair * (2 * ST) + E_OUT + ST * (m // 4) + t + 1)
                            act.wait_ge(s_ssq, pair * (2 * ST) + ST + ST * (m // 4) + t)
                            act.activation(squares[:, 0:NB], resid[:, t, bass.ds(pair * (2 * NB) + (m // 4) * NB, NB)], ACT.Square,
                                           accum_out=r_part[:, t, bass.ds(pair * 2 + m // 4, 1)]).then_inc(s_ssq, 1)
            for t in range(ST):
                turned_hi(1, t)

            def act_gate_up(c, j):
                unit = c * (U_CHUNK // 2) + j + U_FF // 2
                round_unit(unit + 1, 0)
                act.activation(silu_g[:, :], bank[:, 0, :], ACT.Silu).then_inc(s_act_out, 1)
                round_unit(unit + 1, 1)
                act.wait_ge(s_emptied, c * E_CHUNK + j + E_FF + 1)
                act.activation(hid_hi[:, bass.ds(j, 1), :].rearrange("p a s -> p (a s)"), hidden[:, :], ACT.Copy).then_inc(s_hid_hi, 1)

            def act_down(c, d, last=False):
                for m in range(6):
                    if last and m >= 4:
                        continue
                    size = DOWN_UNITS[2] * NB if m % 3 == 0 else UNIT
                    round_unit(c * (U_CHUNK // 2) + d * 3 + U_FF // 2 + CF + 1 + m // 2, m % 2, size)

            def act_chunk(c, last=False):
                with act.Fori(0, CF) as j:
                    act_gate_up(c, j)
                if last:
                    for d in range(OUT_BLOCKS // 2):
                        act_down(c, d, last=d == OUT_BLOCKS // 2 - 1)
                else:
                    with act.Fori(0, OUT_BLOCKS // 2) as d:
                        act_down(c, d)

            with act.Fori(0, CHUNKS - 1) as c:
                act_chunk(c)
            act_chunk(CHUNKS - 1, last=True)

        @block.vector
        def _(dve):
            def low_unit(half, parity, size=UNIT):
                dve.wait_ge(s_whi, half * 2 + parity + 1)
                dve.tensor_tensor(w_lo[:, parity, 0:size], w_raw[:, parity, 0:size],
                                  w_hi[:, parity, 0:size].bitcast(F32), ALU.subtract).then_inc(s_wlo, 1)

            def scale_rows(phase, t):
                g = ST * phase + t
                dve.wait_ge(s_rstd, 2 * g + 2)
                if t >= 2:
                    dve.wait_ge(s_turned, 4 * (g - 1))
                dve.scalar_tensor_tensor(out=scaled[:, t % 2, :], in0=(x_nat, resid)[phase][:, t, :],
                                         scalar=x_rstd[:, phase, t:t + 1], in1=norm_w[:, :],
                                         op0=ALU.mult, op1=ALU.mult).then_inc(s_scaled, 1)

            def turned_lo(phase, t):
                for b in range(4):
                    dve.wait_ge(s_act_hi, 4 * (ST * phase + t) + b + 1)
                    src = bank[:, NORM_BANKS[phase] + b, :].rearrange("p (k s) -> p k s", s=P)
                    tile = (slice(None), slice(4 * b, 4 * b + 4), slice(t * P, (t + 1) * P))
                    dve.tensor_tensor(act_lo[tile], src, act_hi[tile].bitcast(F32), ALU.subtract).then_inc(s_emptied, 1)

            dve.memset(gated[:, 0:CONV_K - 1], 0.0).then_inc(s_pad, 1)
            dve.wait_ge(s_norm_w, 16)
            scale_rows(0, 0)
            for t in range(ST):
                if t + 1 < ST:
                    scale_rows(0, t + 1)
                turned_lo(0, t)
                if t < 2:
                    low_unit(0, t)
            dve.wait_ge(s_rows_t, 1)
            dve.tensor_copy(taps[:, :], bank[:, 4, 0:CONV_K * HEADS + 1]).then_inc(s_taps, 1)
            dve.wait_ge(s_consts, 16 * CONSTS)
            dve.tensor_tensor(lam_in[:, 0:4:2, :], lam_in[:, 0:4:2, :], lam_in[:, 1:4:2, :], ALU.mult).then_inc(s_lam, 1)
            dve.wait_ge(s_lam, 1)
            dve.tensor_reduce(lam_sum[:, :], lam_in[:, 0:4:2, :], AX.X, ALU.add).then_inc(s_lam, 1)
            dve.wait_ge(s_lam_exp, 1)
            dve.tensor_scalar(neg_lam[:, 0:1], lam_exp[:, 1:2], -LAMBDA_INIT, None, ALU.add).then_inc(s_lam, 1)
            dve.wait_ge(s_lam, 3)
            dve.tensor_tensor(neg_lam[:, 1:2], neg_lam[:, 0:1], lam_exp[:, 0:1], ALU.subtract).then_inc(s_lam, 1)
            dve.wait_ge(s_lam, 4)

            def prep_mean_square(head, part):
                dve.wait_ge(s_prep, head * (2 * PREP) + part * PREP + 2)
                dve.tensor_reduce(qk_ssq[:, :], rot_tmp[:, :, :].rearrange("p t (c e) -> p (t c) e", c=2),
                                  AX.X, ALU.add).then_inc(s_prep_ms, 1)
                dve.wait_ge(s_prep_ms, head * 4 + 2 * part + 1)
                dve.tensor_scalar(qk_ms[:, :], qk_ssq[:, :], 1.0 / DK, EPS, ALU.mult, ALU.add).then_inc(s_prep_ms, 1)

            with dve.Fori(0, QKV_BLOCKS // 2) as pair:
                for m in range(8):
                    if m % 4 == 3:
                        sub = m // 4
                        for t in range(ST):
                            if t < ST - 1:
                                dve.wait_ge(s_tile, pair * (2 * (ST - 1)) + (ST - 1) * sub + t + 1)
                            else:
                                dve.wait_ge(s_used, pair * 8 + m + 1)
                            dve.tensor_copy(qkv[:, t, bass.ds(pair * (2 * NB) + sub * NB, NB)],
                                            bank[:, BLOCK_BANKS[sub][t], :]).then_inc(s_emptied, 1)
                    low_unit(pair * 4 + U_QKV // 2 + 1 + m // 2, m % 2)
            prep_mean_square(0, 0)
            prep_mean_square(0, 1)

            def softmax_peak(head, i):
                e, n = i % 2, (i + 1) * P
                banks = slice(SCORE_BANK[e], SCORE_BANK[e] + 2)
                dve.wait_ge(s_scores, head * 4 + i + 1)
                dve.memset(bank[0:CHUNK, banks, n - CHUNK:n], MASKED).then_inc(s_mask, 1)
                dve.wait_ge(s_mask, head * 4 + i + 1)
                dve.tensor_reduce(peak[:, e, :], bank[:, banks, 0:n], AX.X, ALU.max).then_inc(s_peak, 1)
                dve.wait_ge(s_peak, head * 4 + i + 1)
                dve.tensor_scalar(neg_peak[:, e, :], peak[:, e, :], -SCALE, None, ALU.mult).then_inc(s_neg, 1)

            def softmax_combine(head, i):
                e, n = i % 2, (i + 1) * P
                dve.wait_ge(s_exp, head * 8 + 2 * i + 2)
                dve.reciprocal(share[:, e, :], total[:, e, :]).then_inc(s_share, 1)
                dve.wait_ge(s_share, head * 12 + 3 * i + 1)
                dve.tensor_scalar(expo[:, e, 0, 0:n], expo[:, e, 0, 0:n], share[:, e, 0:1], None, ALU.mult).then_inc(s_share, 1)
                dve.tensor_tensor(share[:, e, 1:2], share[:, e, 1:2], neg_lam[:, 1:2], ALU.mult).then_inc(s_share, 1)
                dve.wait_ge(s_share, head * 12 + 3 * i + 3)
                dve.scalar_tensor_tensor(out=expo[:, e, 0, 0:n], in0=expo[:, e, 1, 0:n], scalar=share[:, e, 1:2],
                                         in1=expo[:, e, 0, 0:n], op0=ALU.mult, op1=ALU.add).then_inc(s_probs, 1)

            def dve_head(pair, sub, last=False):
                head = pair * 2 + sub
                conv_out = mixed[:, bass.ds(head + HEADS, 1), :].rearrange("p a s -> p (a s)")

                def tap(j):
                    return taps[:, bass.ds(head + j * HEADS, 1)]

                for s in range(SLOTS):
                    if s == 16:
                        dve.wait_ge(s_act_out, head + 1)
                        dve.wait_ge(s_used, head * 3 + U_HEAD + 2)
                        u = gated[:, CONV_K - 1:CONV_K - 1 + SEQ]
                        dve.tensor_tensor(u, u, bank[:, CONV_BANK[1], :], ALU.mult).then_inc(s_emptied, 1)
                    if s % 8 == 0 and s > 0:
                        m = 3 * sub + s // 8 - 1
                        low_unit(pair * 3 + U_HEAD // 2 + 1 + m // 2, m % 2)
                    if s - 1 in SCORES_AT:
                        softmax_peak(head, SCORES_AT[s - 1])
                    if s - 3 in SCORES_AT:
                        softmax_combine(head, SCORES_AT[s - 3])
                    if s - 1 in PLACE_AT:
                        i = PLACE_AT[s - 1]
                        dve.wait_ge(s_oturn, head * 4 + i + 1)
                        dve.tensor_scalar(mixed[:, bass.ds(head, 1), i * P:(i + 1) * P].rearrange("p a s -> p (a s)"),
                                          bank[:, VALUE_BANK, 0:P], taps[:, CONV_K * HEADS:CONV_K * HEADS + 1],
                                          1.0 - LAMBDA_INIT, ALU.mult, ALU.mult).then_inc(s_placed, 1)
                    if s in (2, 11) and not last:
                        prep_mean_square(head + 1, s // 9)
                    if 18 <= s < 18 + CONV_K:
                        j = s - 18
                        shift = gated[:, CONV_K - 1 - j:CONV_K - 1 - j + SEQ]
                        if j == 0:
                            dve.wait_ge(s_emptied, head * 2 + E_HEAD + 1)
                            dve.tensor_scalar(conv_out, shift, tap(CONV_K - 1), None, ALU.mult).then_inc(s_conv, 1)
                        else:
                            dve.wait_ge(s_conv, head * CONV_K + j)
                            dve.scalar_tensor_tensor(out=conv_out, in0=shift, scalar=tap(CONV_K - 1 - j), in1=conv_out,
                                                     op0=ALU.mult, op1=ALU.add).then_inc(s_conv, 1)
                dve.wait_ge(s_conv, head * CONV_K + CONV_K)
                dve.wait_ge(s_used, head * 3 + U_HEAD + 3)
                dve.tensor_tensor(conv_out, bank[:, CONV_BANK[2], :], conv_out, ALU.mult).then_inc(s_emptied, 1)
                m = 3 * sub + 2
                low_unit(pair * 3 + U_HEAD // 2 + 1 + m // 2, m % 2)

            with dve.Fori(0, HEADS // 2 - 1) as pair:
                dve_head(pair, 0)
                dve_head(pair, 1)
            dve_head(HEADS // 2 - 1, 0)
            dve_head(HEADS // 2 - 1, 1, last=True)

            for k in range(KT):
                dve.wait_ge(s_mix_hi, k + 1)
                dve.tensor_tensor(act_lo[:, k, :], mixed[:, k, :], act_hi[:, k, :].bitcast(F32), ALU.subtract).then_inc(s_low, 1)

            def add_tile(columns, b, t):
                dve.tensor_tensor(resid[:, t, columns], bank[:, b, :], resid[:, t, columns], ALU.add).then_inc(s_emptied, 1)

            dve.wait_ge(s_resid, 16)
            with dve.Fori(0, OUT_BLOCKS // 2) as pair:
                for m in range(8):
                    if m % 4 == 3:
                        sub = m // 4
                        for t in range(ST):
                            if t < ST - 1:
                                dve.wait_ge(s_tile, pair * (2 * (ST - 1)) + T_OUT + (ST - 1) * sub + t + 1)
                            else:
                                dve.wait_ge(s_used, pair * 8 + U_OUT + m + 1)
                            add_tile(bass.ds(pair * (2 * NB) + sub * NB, NB), BLOCK_BANKS[sub][t], t)
                    low_unit(pair * 4 + U_OUT // 2 + 1 + m // 2, m % 2)

            def resid_ssq(t):
                dve.wait_ge(s_ssq, ST + ST * (OUT_BLOCKS - 1) + t + 1)
                dve.tensor_reduce(r_ssq[:, t:t + 1], r_part[:, t, :], AX.X, ALU.add).then_inc(s_rsum, 1)

            for t in range(ST):
                resid_ssq(t)
            dve.wait_ge(s_norm_w2, 16)
            scale_rows(1, 0)
            for t in range(ST):
                if t + 1 < ST:
                    scale_rows(1, t + 1)
                turned_lo(1, t)

            def dve_gate_up(c, j):
                unit = c * (U_CHUNK // 2) + j + U_FF // 2
                low_unit(unit + 1, 0)
                dve.wait_ge(s_act_out, c * CF + j + HEADS + 1)
                dve.wait_ge(s_used, unit * 2 + 2)
                dve.wait_ge(s_low, c * CF + KT + j)
                dve.tensor_tensor(hidden[:, :], bank[:, 1, :], silu_g[:, :], ALU.mult).then_inc(s_emptied, 1)
                low_unit(unit + 1, 1)
                dve.wait_ge(s_hid_hi, c * CF + j + 1)
                dve.tensor_tensor(hid_lo[:, bass.ds(j, 1), :].rearrange("p a s -> p (a s)"), hidden[:, :],
                                  hid_hi[:, bass.ds(j, 1), :].rearrange("p a s -> p (a s)").bitcast(F32),
                                  ALU.subtract).then_inc(s_low, 1)

            def dve_down(c, d, last=False):
                for m in range(6):
                    sub, part = divmod(m, 3)
                    unit = c * (U_CHUNK // 2) + d * 3 + U_FF // 2 + CF + m // 2
                    if part == 2:
                        for t in range(ST):
                            if t < ST - 1:
                                dve.wait_ge(s_tile, c * T_CHUNK + d * (2 * (ST - 1)) + T_FF + (ST - 1) * sub + t + 1)
                            else:
                                dve.wait_ge(s_used, unit * 2 + m % 2 + 1)
                            add_tile(bass.ds(d * (2 * NB) + sub * NB, NB), DOWN_BANKS[sub][t], t)
                    if not (last and m >= 4):
                        low_unit(unit + 1, m % 2, DOWN_UNITS[2] * NB if part == 0 else UNIT)

            def dve_chunk(c, last=False):
                with dve.Fori(0, CF) as j:
                    dve_gate_up(c, j)
                if last:
                    for d in range(OUT_BLOCKS // 2):
                        dve_down(c, d, last=d == OUT_BLOCKS // 2 - 1)
                else:
                    with dve.Fori(0, OUT_BLOCKS // 2) as d:
                        dve_down(c, d)

            with dve.Fori(0, CHUNKS - 1) as c:
                dve_chunk(c)
            dve_chunk(CHUNKS - 1, last=True)

        @block.tensor
        def _(pe):
            def product(dst, left, right, start, stop):
                pe.matmul(dst, left[0], right[0], start=start, stop=False)
                pe.matmul(dst, left[0], right[1], start=False, stop=False)
                return pe.matmul(dst, left[1], right[0], start=False, stop=stop)

            def turn_rows(phase, t):
                g = ST * phase + t
                pe.wait_ge(s_scaled, g + 1)
                for b in range(4):
                    if t > 0:
                        pe.wait_ge(s_emptied, (0, E_NORM2)[phase] + 4 * (t - 1) + b + 1)
                    for k in range(4):
                        ins = pe.transpose(bank[:, NORM_BANKS[phase] + b, k * P:(k + 1) * P],
                                           scaled[:, t % 2, (4 * b + k) * P:(4 * b + k + 1) * P], ident[:, :])
                    ins.then_inc(s_turned, 1)

            def block_unit(half, m, banks, tiles, free, parts=UK, units=4):
                pe.wait_ge(s_wlo, half * 2 + m % 2 + 1)
                for t in range(ST):
                    if m % units == 0:
                        pe.wait_ge(s_emptied, free(t))
                    for k in range(parts):
                        first, last = m % units == 0 and k == 0, m % units == units - 1 and k == parts - 1
                        ins = product(bank[:, banks[t], :], tiles(k, t),
                                      (moving(w_hi, m % 2)[:, k, :], moving(w_lo, m % 2)[:, k, :]), first, last)
                    if m % units == units - 1 and t < ST - 1:
                        ins.then_inc(s_tile, 1)
                ins.then_inc(s_used, 1)

            def act_tiles(m):
                return lambda k, t: tuple(a[:, UK * m + k, t * P:(t + 1) * P] for a in (act_hi, act_lo))

            pe.wait_ge(s_ident, 2)
            for t in range(ST):
                turn_rows(0, t)
            pe.wait_ge(s_consts, 16 * CONSTS)
            pe.wait_ge(s_emptied, E_QKV)
            pe.transpose(bank[:, 4, 0:CONV_K * HEADS + 1], rows[0:CONV_K * HEADS + 1, :],
                         ident[0:CONV_K * HEADS + 1, 0:CONV_K * HEADS + 1]).then_inc(s_rows_t, 1)
            pe.wait_ge(s_taps, 1)

            with pe.Fori(0, QKV_BLOCKS // 2) as pair:
                for m in range(8):
                    sub = m // 4
                    block_unit(pair * 4 + m // 2, m, BLOCK_BANKS[sub], act_tiles(m % 4),
                               lambda t: pair * (2 * ST) + E_QKV + ST * (sub - 2) + t + 1)

            def qk_turn(head, part):
                pe.wait_ge(s_prep, head * (2 * PREP) + (part + 1) * PREP + 1)
                if part == 1:
                    pe.wait_ge(s_qk_t, head * 2 + 1)
                for t in range(ST):
                    ins = pe.transpose(bank[:, TURN_BANK, t * P:(t + 1) * P], rot[:, part, t, :], ident[:, :])
                ins.then_inc(s_qk_turn, 1)

            def scores(head, i):
                if i == 0:
                    pe.wait_ge(s_qk_t, head * 2 + 2)
                if i >= 2:
                    pe.wait_ge(s_exp, head * 8 + 2 * (i - 2) + 2)
                for c in range(2):
                    rows_ = slice(c * DK, (c + 1) * DK)
                    ins = pe.matmul(bank[:, SCORE_BANK[i % 2] + c, 0:(i + 1) * P], q_t[rows_, i * P:(i + 1) * P],
                                    k_t[rows_, 0:(i + 1) * P], start=True, stop=True)
                ins.then_inc(s_scores, 1)

            def turn_probs(head, i):
                pe.wait_ge(s_probs, head * 4 + i + 1)
                for b in range(i + 1):
                    ins = pe.transpose(bank[:, TURN_BANK, b * P:(b + 1) * P], expo[:, i % 2, 0, b * P:(b + 1) * P], ident[:, :])
                ins.then_inc(s_pturn, 1)

            def values(head, i):
                pe.wait_ge(s_probs_t, head * 4 + i + 1)
                if i > 0:
                    pe.wait_ge(s_placed, head * 4 + i)
                for b in range(i + 1):
                    ins = pe.matmul(bank[:, VALUE_BANK, 0:DV], probs_t[:, b * P:(b + 1) * P],
                                    qkv[:, b, bass.ds(head * DV + 2 * HEADS * DV, DV)], start=b == 0, stop=b == i)
                ins.then_inc(s_values, 1)

            def turn_attn(head, i):
                pe.wait_ge(s_attn_n, head * 4 + i + 1)
                pe.transpose(bank[:, VALUE_BANK, 0:P], attn_n[:, :], ident[:, :]).then_inc(s_oturn, 1)

            def pe_head(pair, sub, last=False):
                head = pair * 2 + sub
                for s in range(SLOTS):
                    part = s // 8
                    m = 3 * sub + part
                    b = bank[:, CONV_BANK[part], :]
                    if s % 8 == 0:
                        pe.wait_ge(s_wlo, pair * 6 + U_HEAD + m + 1)
                        if part == 0:
                            pe.wait_ge(s_emptied, head * 2 + E_HEAD)
                        elif part == 2:
                            pe.wait_ge(s_act_out, head + 1)
                    if s in SCORES_AT:
                        scores(head, SCORES_AT[s])
                    if s in TURN_AT:
                        turn_probs(head, TURN_AT[s])
                    if s in VALUES_AT:
                        values(head, VALUES_AT[s])
                    if s in PLACE_AT:
                        turn_attn(head, PLACE_AT[s])
                    if s in QK_TURN_AT and not last:
                        qk_turn(head + 1, QK_TURN_AT[s])
                    for k in range(2 * (s % 8), 2 * (s % 8) + 2):
                        ins = product(b, (stationary(w_hi, m % 2)[:, k, :], stationary(w_lo, m % 2)[:, k, :]),
                                      (act_hi[:, k, :], act_lo[:, k, :]), k == 0, k == KT - 1)
                    if s % 8 == 7:
                        ins.then_inc(s_used, 1)

            pe.wait_ge(s_emptied, E_HEAD)
            for part in range(2):
                qk_turn(0, part)
            with pe.Fori(0, HEADS // 2 - 1) as pair:
                pe_head(pair, 0)
                pe_head(pair, 1)
            pe_head(HEADS // 2 - 1, 0)
            pe_head(HEADS // 2 - 1, 1, last=True)

            with pe.Fori(0, OUT_BLOCKS // 2) as pair:
                for m in range(8):
                    sub = m // 4
                    pe.wait_ge(s_low, UK * (m % 4) + UK)
                    block_unit(pair * 4 + U_OUT // 2 + m // 2, m, BLOCK_BANKS[sub], act_tiles(m % 4),
                               lambda t: pair * (2 * ST) + E_OUT + ST * (sub - 2) + t + 1)

            for t in range(ST):
                turn_rows(1, t)
            pe.wait_ge(s_emptied, E_FF)

            def pe_gate_up(c, j):
                unit = c * (U_CHUNK // 2) + j + U_FF // 2
                for parity in range(2):
                    pe.wait_ge(s_wlo, unit * 2 + parity + 1)
                    if parity == 0:
                        pe.wait_ge(s_act_out, c * CF + j + HEADS)
                        pe.wait_ge(s_emptied, c * E_CHUNK + j + E_FF - ST)
                    else:
                        pe.wait_ge(s_emptied, c * E_CHUNK + j + E_FF)
                    for k in range(KT):
                        ins = product(bank[:, parity, :],
                                      (stationary(w_hi, parity)[:, k, :], stationary(w_lo, parity)[:, k, :]),
                                      (act_hi[:, k, :], act_lo[:, k, :]), k == 0, k == KT - 1)
                    ins.then_inc(s_used, 1)

            def pe_down(c, d):
                for m in range(6):
                    sub, part = divmod(m, 3)
                    first = UK * part
                    pe.wait_ge(s_low, c * CF + KT + first + DOWN_UNITS[part])
                    down_unit(c, d, m, sub, part, first)

            def down_unit(c, d, m, sub, part, first):
                half = c * (U_CHUNK // 2) + d * 3 + U_FF // 2 + CF + m // 2
                pe.wait_ge(s_wlo, half * 2 + m % 2 + 1)
                for t in range(ST):
                    if part == 0:
                        pe.wait_ge(s_emptied, c * E_CHUNK + d * (2 * ST) + E_FF + CF + ST * (sub - 2) + (t + 1 if t < 2 or sub else ST + ST))
                    for k in range(DOWN_UNITS[part]):
                        ins = product(bank[:, DOWN_BANKS[sub][t], :],
                                      tuple(a[:, first + k, t * P:(t + 1) * P] for a in (hid_hi, hid_lo)),
                                      (moving(w_hi, m % 2)[:, k, :], moving(w_lo, m % 2)[:, k, :]),
                                      part == 0 and k == 0, part == 2 and k == DOWN_UNITS[part] - 1)
                    if part == 2 and t < ST - 1:
                        ins.then_inc(s_tile, 1)
                ins.then_inc(s_used, 1)

            with pe.Fori(0, CHUNKS) as c:
                with pe.Fori(0, CF) as j:
                    pe_gate_up(c, j)
                with pe.Fori(0, OUT_BLOCKS // 2) as d:
                    pe_down(c, d)


_INS = ["x", "attn_norm_w", "w_in", "q_norm_w", "k_norm_w", "lambda_q1", "lambda_k1", "lambda_q2", "lambda_k2",
        "subln_w", "conv_w", "w_out", "ffn_norm_w", "w_gate", "w_up", "w_down"]


def kernel(**inputs):
    import numpy as _np
    import concourse.bacc as _bacc
    from concourse import mybir as _mybir
    from concourse.bass_utils import run_bass_kernel_spmd as _run

    nc = _bacc.Bacc("TRN2", target_bir_lowering=False, num_devices=1, dynamic_dma_scratch_size=1024)
    arrays, args = {}, []
    for name in _INS:
        a = _np.ascontiguousarray(inputs[name])
        arrays[f"in_{name}_dram"] = a
        args.append(nc.dram_tensor(f"in_{name}_dram", a.shape, _mybir.dt.from_np(a.dtype), kind="ExternalInput").ap())
    tables = rope_tables()
    arrays["rope_dram"] = tables
    args.append(nc.dram_tensor("rope_dram", tables.shape, F32, kind="ExternalInput").ap())
    args.append(nc.dram_tensor("out_dram", (1, SEQ, D), F32, kind="ExternalOutput").ap())
    build(nc, *args)
    r = _run(nc, [arrays], core_ids=[0])
    return r.results[0]["out_dram"]
```

```python
import numpy as np
import concourse.bass as bass
from concourse import mybir

F32, F32R = mybir.dt.float32, mybir.dt.float32r
ALU = mybir.AluOpType
ACT = mybir.ActivationFunctionType
AX = mybir.AxisListType

P = 128
D = 2048
SEQ = 512
HEADS = 8
DK = 64
DV = 128
FF = 5632
CHUNK = 64
CONV_K = 3
EPS = 1e-6
SUBLN_EPS = 1e-5
LAMBDA_INIT = 0.8 - 0.6 * float(np.exp(0.0))
ROPE_THETA = 10000.0
SCALE = DK ** -0.5
MASKED = -1e30

ST = SEQ // P
KT = D // P
NB = 512
UK = 4
UNIT = UK * NB
QKV_BLOCKS = 3 * HEADS * DV // NB
OUT_BLOCKS = D // NB
CONV_COLS = 3 * HEADS * DV
FT = FF // P
CHUNKS = 4
CF = FT // CHUNKS
DOWN_UNITS = (4, 4, 3)
assert sum(DOWN_UNITS) == CF

U_QKV = 0
U_HEAD = U_QKV + QKV_BLOCKS * KT // UK
U_OUT = U_HEAD + 3 * HEADS
U_FF = U_OUT + OUT_BLOCKS * KT // UK
U_CHUNK = 2 * CF + OUT_BLOCKS * len(DOWN_UNITS)

E_QKV = ST * KT // 4
E_HEAD = E_QKV + ST * QKV_BLOCKS
E_OUT = E_HEAD + 2 * HEADS
E_NORM2 = E_OUT + ST * OUT_BLOCKS
E_FF = E_NORM2 + ST * KT // 4
E_CHUNK = CF + ST * OUT_BLOCKS

T_OUT = (ST - 1) * QKV_BLOCKS
T_FF = T_OUT + (ST - 1) * OUT_BLOCKS
T_CHUNK = (ST - 1) * OUT_BLOCKS

PREP = 8
CONSTS = 7

E_END = E_FF + CHUNKS * E_CHUNK

SLOTS = 24
SCORES_AT = {0: 0, 4: 1, 8: 2, 12: 3}
TURN_AT = {5: 0, 9: 1, 13: 2, 17: 3}
VALUES_AT = {6: 0, 10: 1, 14: 2, 18: 3}
PLACE_AT = {9: 0, 13: 1, 17: 2, 21: 3}
QK_TURN_AT = {19: 0, 21: 1}
ROUND_AT = (3, 11, 19)
POOL_ORDER = ("q0", "q1", "q2", "q3", "q4", "r0", "q5", "q6", "q7", "k0", "r1", "k1", "k2", "k3", "r2",
              "k4", "k5", "k6", "k7", "r3")

WARM_STEPS = 14
BASE = 1152


def rope_tables():
    freq = (ROPE_THETA ** (-np.arange(0, DK, 2, dtype=np.float32) / np.float32(DK))).astype(np.float32)
    angle = np.arange(SEQ, dtype=np.float32)[:, None] * freq[None, :]
    both = np.stack([np.cos(angle), np.sin(angle)]).astype(np.float32)
    return np.ascontiguousarray(both.reshape(2, ST, P, DK // 2).transpose(2, 0, 1, 3))


def build(nc, x, attn_norm_w, w_in, q_norm_w, k_norm_w, lambda_q1, lambda_k1, lambda_q2, lambda_k2,
          subln_w, conv_w, w_out, ffn_norm_w, w_gate, w_up, w_down, rope_cs, out):
    K = 1024
    cursor = [BASE]

    def region(size):
        start = cursor[0]
        cursor[0] += size
        return start

    def at(name, offset, shape, dt=F32):
        return nc.alloc_sbuf_tensor_at(name, shape, dt, offset=offset)

    act_hi = at("act_hi", region(32 * K), [P, KT, SEQ], F32R)
    act_lo = at("act_lo", region(32 * K), [P, KT, SEQ], F32R)
    w_raw = at("w_raw", region(16 * K), [P, 2, UNIT])
    w_hi = at("w_hi", region(16 * K), [P, 2, UNIT], F32R)
    w_lo = at("w_lo", region(16 * K), [P, 2, UNIT], F32R)
    wide = region(48 * K)
    qkv = at("qkv", wide, [P, ST, 3 * HEADS * DV])
    norm_w = at("norm_w", wide, [P, D])
    scaled = at("scaled", wide + 8 * K, [P, 2, D])
    squares = at("squares", wide + 24 * K, [P, D])
    hid_hi = at("hid_hi", wide, [P, CF, SEQ], F32R)
    hid_lo = at("hid_lo", wide + 2 * CF * K, [P, CF, SEQ], F32R)
    tall = region(32 * K)
    x_nat = at("x_nat", tall, [P, ST, D])
    mixed = at("mixed", tall, [P, KT, SEQ])
    resid = at("resid", tall, [P, ST, D])
    work = region(18 * K + 768)
    turned = region(8 * K)
    expo = at("expo", work, [P, 2, 2, NB])
    probs_t = at("probs_t", work + 8 * K, [P, NB])
    q_t = at("q_t", turned, [P, 2, SEQ], F32R)
    k_t = at("k_t", turned + 4 * K, [P, 2, SEQ], F32R)
    k_t_lo = at("k_t_lo", work + 10 * K, [P, 2, SEQ], F32R)
    rot = (at("rot_q", work + 14 * K, [P, ST, DV]), at("rot_k", tall + (HEADS - 1) * 2 * K, [P, ST, DV]))
    rot_tmp = at("rot_tmp", tall + (KT - 1) * 2 * K, [P, ST, DV])
    gated = at("gated", work + 16 * K, [P, SEQ + CONV_K])
    attn_n = at("attn_n", work + 18 * K + 256, [P, DV])
    silu_g = at("silu_g", work, [P, SEQ])
    hidden = at("hidden", work + 2 * K, [P, SEQ])
    small = region(3 * K)
    at_small = [small]

    def col(name, shape):
        n = 4 * int(np.prod(shape[1:]))
        t = at(name, at_small[0], shape)
        at_small[0] += -(-n // 32) * 32
        assert at_small[0] <= small + 3 * K
        return t

    ident = col("ident", [P, P])
    cs = col("cs", [P, 2, ST, DK // 2])
    qk_w = col("qk_w", [P, 2, DK])
    lam_in = at("lam_in", work + K, [P, 4, DK])
    rows = at("rows", work, [CONV_K * HEADS + 1, P])
    taps = col("taps", [P, CONV_K * HEADS + 1])
    lam_sum = col("lam_sum", [P, 2])
    lam_exp = col("lam_exp", [P, 2])
    neg_lam = col("neg_lam", [P, 2])
    half_power = col("half_power", [P, 8])
    x_ssq = col("x_ssq", [P, ST])
    x_rstd = col("x_rstd", [P, 2, ST])
    r_part = col("r_part", [P, ST, OUT_BLOCKS])
    r_ssq = col("r_ssq", [P, ST])
    qk_ssq = col("qk_ssq", [P, 2 * ST])
    qk_ms = col("qk_ms", [P, 2 * ST])
    qk_rstd = col("qk_rstd", [P, 2 * ST])
    peak = col("peak", [P, 2, 2])
    neg_peak = col("neg_peak", [P, 2, 2])
    total = col("total", [P, 2, 2])
    share = col("share", [P, 2, 2])
    o_ssq = col("o_ssq", [P, 2])
    o_ms = col("o_ms", [P, 2])
    o_rstd = col("o_rstd", [P, 2])
    assert cursor[0] <= nc.sbuf_usable_end

    bank = nc.alloc_psum_tensor("bank", [P, 8, NB], F32)
    SCORE_BANK = (4, 2)
    TURN_BANK, VALUE_BANK = 6, 7
    QK_BANKS = (2, 3)
    NORM_BANK = ((4, 4, 4, 4), (4, 0, 4, 4))
    TAPS_BANK = 3
    DOWN_BANKS = ((2, 3, 0, 1), (4, 5, 6, 7))

    sem = nc.alloc_semaphore
    s_consts = sem("consts_loaded")
    s_norm_w = sem("norm_w_loaded")
    s_rows = sem("taps_rows_loaded")
    s_x = [sem(f"x_loaded{t}") for t in range(ST)]
    s_resid = sem("resid_loaded")
    s_norm_w2 = sem("norm_w2_loaded")
    s_raw = [sem(f"w_raw_loaded{p}") for p in range(2)]
    s_out = sem("out_written")
    s_ident = sem("ident_made")
    s_half = sem("half_power_made")
    s_ssq = sem("row_ssq_made")
    s_rsum = sem("resid_ssq_made")
    s_rstd = sem("row_rstd_steps")
    s_scaled = sem("row_scaled")
    s_turned = sem("act_turned")
    s_act_hi = sem("act_hi_made")
    s_rows_t = sem("rows_turned")
    s_taps = sem("taps_made")
    s_lam = sem("lambda_steps")
    s_lam_exp = sem("lambda_exp")
    s_whi = sem("w_hi_made")
    s_wlo = sem("w_lo_made")
    s_used = sem("w_used")
    s_tile = sem("tile_sum")
    s_emptied = sem("emptied")
    s_silu = sem("silu_table_used")
    s_act_out = sem("act_emptied")
    s_prep = sem("prep_steps")
    s_prep_ms = sem("prep_mean_square")
    s_qk_in = sem("qk_copied")
    s_qk_turn = sem("qk_turned")
    s_qk_t = sem("qk_t_hi_ready")
    s_qk_lo = sem("qk_t_lo_ready")
    s_scores = sem("scores_ready")
    s_mask = sem("scores_masked")
    s_peak = sem("peak_found")
    s_neg = sem("neg_peak_made")
    s_exp = sem("exp_made")
    s_share = sem("share_steps")
    s_probs = sem("probs_ready")
    s_pturn = sem("probs_turned")
    s_probs_t = sem("probs_t_ready")
    s_values = sem("values_summed")
    s_ossq = sem("attn_mean_square")
    s_orstd = sem("attn_rstd")
    s_attn_n = sem("attn_normed")
    s_oturn = sem("attn_turned")
    s_placed = sem("attn_placed")
    s_pad = sem("zeros_made")
    s_conv = sem("conv_steps")
    s_mix_hi = sem("mixed_hi_made")
    s_low = sem("operand_lo_made")
    s_hid_hi = sem("hidden_hi_made")

    w_in_v = w_in[0].rearrange("(k p) n -> p k n", p=P)
    w_out_v = w_out[0].rearrange("(k p) n -> p k n", p=P)
    w_gate_v = w_gate[0].rearrange("(k p) n -> p k n", p=P)
    w_up_v = w_up[0].rearrange("(k p) n -> p k n", p=P)
    w_down_v = w_down[0].rearrange("(k p) n -> p k n", p=P)
    x_v = x[0].rearrange("(t p) d -> p t d", p=P)
    out_v = out[0].rearrange("(t p) d -> p t d", p=P)

    def moving(w, slot):
        return w[:, slot, :].rearrange("p (k n) -> p k n", n=NB)

    def stationary(w, slot):
        return w[:, slot, :].rearrange("p (k n) -> p k n", n=P)

    def half_rows(c):
        return slice(c * DK, (c + 1) * DK)

    block = nc.Block()
    with block:

        @block.sync
        def _(sp):
            def load(half, parity, source, first=False):
                rows_, columns = source.shape[1], source.shape[2]
                if not first:
                    sp.wait_ge(s_wlo, half * 4 + 2 * parity - 2)
                dst = w_raw[:, parity, 0:rows_ * columns].rearrange("p (k n) -> p k n", n=columns)
                sp.dma_start(dst, source).then_inc(s_raw[parity], 16)

            def qkv_source(blk, m):
                return w_in_v[:, UK * m:UK * m + UK, bass.ds(blk * NB, NB)]

            sp.dma_start(x_nat[:, 0, :], x_v[:, 0, :]).then_inc(s_x[0], 16)
            sp.dma_start(norm_w[:, :], attn_norm_w[0, :].partition_broadcast(P)).then_inc(s_norm_w, 16)
            load(0, 0, qkv_source(0, 0), first=True)
            load(0, 1, qkv_source(0, 1), first=True)
            sp.dma_start(x_nat[:, 1, :], x_v[:, 1, :]).then_inc(s_x[1], 16)
            sp.dma_start(x_nat[:, 2, :], x_v[:, 2, :]).then_inc(s_x[2], 16)
            sp.dma_start(x_nat[:, 3, :], x_v[:, 3, :]).then_inc(s_x[3], 16)
            load(1, 0, qkv_source(0, 2))
            load(1, 1, qkv_source(0, 3))
            with sp.Fori(1, QKV_BLOCKS) as blk:
                for m in range(4):
                    load(blk * 2 + m // 2, m % 2, qkv_source(blk, m))
            with sp.Fori(0, HEADS // 2) as pair:
                for m in range(6):
                    sub, part = divmod(m, 3)
                    column = CONV_COLS + (1, 2, 0)[part] * HEADS * DV + sub * DV
                    load(pair * 3 + U_HEAD // 2 + m // 2, m % 2,
                         w_in_v[:, :, bass.ds(pair * (2 * DV) + column, DV)])
            with sp.Fori(0, OUT_BLOCKS) as blk:
                for m in range(4):
                    load(blk * 2 + U_OUT // 2 + m // 2, m % 2,
                         w_out_v[:, UK * m:UK * m + UK, bass.ds(blk * NB, NB)])
            with sp.Fori(0, CHUNKS) as c:
                with sp.Fori(0, CF) as j:
                    unit = c * (U_CHUNK // 2) + j + U_FF // 2
                    column = c * (CF * P) + j * P
                    load(unit, 0, w_gate_v[:, :, bass.ds(column, P)])
                    load(unit, 1, w_up_v[:, :, bass.ds(column, P)])
                with sp.Fori(0, OUT_BLOCKS // 2) as d:
                    for m in range(6):
                        sub, part = divmod(m, 3)
                        load(c * (U_CHUNK // 2) + d * 3 + U_FF // 2 + CF + m // 2, m % 2,
                             w_down_v[:, bass.ds(c * CF + 4 * part, DOWN_UNITS[part]),
                                      bass.ds(d * (2 * NB) + sub * NB, NB)])
            with sp.Fori(0, OUT_BLOCKS) as d:
                for t in range(ST):
                    sp.wait_ge(s_emptied, d * ST + E_END - ST * OUT_BLOCKS + t + 1)
                    sp.dma_start(out_v[:, t, bass.ds(d * NB, NB)],
                                 resid[:, t, bass.ds(d * NB, NB)]).then_inc(s_out, 16)
            sp.wait_ge(s_out, 16 * ST * OUT_BLOCKS)

        @block.gpsimd
        def _(pool):
            pool.memset(ident[:, :], 0.0).then_inc(s_ident, 1)
            pool.memset(half_power[:, :], -0.5).then_inc(s_half, 1)
            pool.wait_ge(s_ident, 1)
            pool.affine_select(out=ident[:, :], in_=ident[:, :], compare_op=ALU.not_equal, fill=1.0, base=0,
                               pattern=[[-1, P]], channel_multiplier=1).then_inc(s_ident, 1)
            pool.wait_ge(s_half, 1)

            def row_rstd(phase, t):
                r, n = x_rstd[:, phase, t:t + 1], 2 * (ST * phase + t)
                if phase == 0:
                    pool.wait_ge(s_ssq, t + 1)
                else:
                    pool.wait_ge(s_rsum, t + 1)
                ssq = (x_ssq, r_ssq)[phase][:, t:t + 1]
                pool.tensor_scalar(r, ssq, 1.0 / D, EPS, ALU.mult, ALU.add).then_inc(s_rstd, 1)
                pool.wait_ge(s_rstd, n + 1)
                pool.tensor_tensor(r, r, half_power[:, 0:1], ALU.pow).then_inc(s_rstd, 1)

            def prep_step(head, part, step):
                new, tmp = rot[part][:, :, :], rot_tmp[:, :, :]
                halves, tmp_halves = (a.rearrange("p t (c e) -> p (t c) e", c=2) for a in (new, tmp))
                quarters, tmp_quarters = (a.rearrange("p t (c e) -> p t c e", c=4) for a in (new, tmp))
                shape, h = [P, ST, 4, DK // 2], DK // 2
                pool.wait_ge(s_prep, head * (2 * PREP) + part * PREP + step + 1)
                if step == 0:
                    pool.wait_ge(s_qk_in, head * 2 + part + 1)
                    ins = pool.tensor_tensor(tmp, new, new, ALU.mult)
                elif step == 1:
                    pool.wait_ge(s_prep_ms, head * 4 + 2 * part + 2)
                    ins = pool.tensor_tensor(qk_rstd[:, :], qk_ms[:, :], half_power[:, :], ALU.pow)
                elif step == 2:
                    rstd = qk_rstd[:, :].rearrange("p (t c) -> p t c", c=2).unsqueeze(3).to_broadcast([P, ST, 2, DK])
                    both = new.rearrange("p t (c e) -> p t c e", c=2)
                    ins = pool.tensor_tensor(both, both, rstd, ALU.mult)
                elif step == 3:
                    weight = qk_w[:, part, :].unsqueeze(1).to_broadcast([P, 2 * ST, DK])
                    ins = pool.tensor_tensor(halves, halves, weight, ALU.mult)
                elif step == 4:
                    ins = pool.tensor_tensor(tmp_quarters, quarters, cs[:, 1, :, :].unsqueeze(2).to_broadcast(shape), ALU.mult)
                elif step == 5:
                    ins = pool.tensor_tensor(quarters, quarters, cs[:, 0, :, :].unsqueeze(2).to_broadcast(shape), ALU.mult)
                elif step == 6:
                    ins = pool.tensor_tensor(halves[:, :, 0:h], halves[:, :, 0:h], tmp_halves[:, :, h:DK], ALU.subtract)
                else:
                    ins = pool.tensor_tensor(halves[:, :, h:DK], halves[:, :, h:DK], tmp_halves[:, :, 0:h], ALU.add)
                ins.then_inc(s_prep, 1)

            def attn_rstd(head, i):
                e = slice(i % 2, i % 2 + 1)
                pool.wait_ge(s_ossq, head * 8 + 2 * i + 2)
                pool.tensor_tensor(o_rstd[:, e], o_ms[:, e], half_power[:, 0:1], ALU.pow).then_inc(s_orstd, 1)

            def pool_head(head, last=False):
                for what, n in POOL_ORDER:
                    if what == "r":
                        attn_rstd(head, int(n))
                    elif not last:
                        prep_step(head + 1, "qk".index(what), int(n))

            for t in range(ST):
                row_rstd(0, t)
            pool.wait_ge(s_consts, 16 * CONSTS)
            pool.memset(qk_rstd[:, :], 0.0).then_inc(s_prep, 1)
            for part in range(2):
                for step in range(PREP):
                    prep_step(0, part, step)
            with pool.Fori(0, HEADS // 2 - 1) as pair:
                pool_head(pair * 2)
                pool_head(pair * 2 + 1)
            pool_head(HEADS - 2)
            pool_head(HEADS - 1, last=True)
            for t in range(ST):
                row_rstd(1, t)

        @block.scalar
        def _(act):
            taps_rows = CONV_K * HEADS
            act.dma_start(rows[0:taps_rows, :], conv_w[0].rearrange("j (h p) -> (j h) p", p=P)).then_inc(s_rows, 16)
            act.dma_start(rows[taps_rows:taps_rows + 1, :], subln_w).then_inc(s_rows, 16)

            def round_unit(half, parity, size=UNIT, first=False, pieces=(0, 1)):
                for q in pieces:
                    if q == 0:
                        act.wait_ge(s_raw[parity], half * 16 + 16)
                        if not first:
                            act.wait_ge(s_used, half * 2 + parity - 1)
                    part = slice(q * size // 2, (q + 1) * size // 2)
                    act.activation(w_hi[:, parity, part], w_raw[:, parity, part], ACT.Copy).then_inc(s_whi, 1)

            def turned_hi(phase, t, banks=range(4)):
                for b in banks:
                    act.wait_ge(s_turned, 4 * (ST * phase + t) + b + 1)
                    src = bank[:, NORM_BANK[phase][t] + b, :].rearrange("p (k s) -> p k s", s=P)
                    act.activation(act_hi[:, 4 * b:4 * b + 4, t * P:(t + 1) * P], src, ACT.Copy).then_inc(s_act_hi, 1)

            def x_square(t):
                act.wait_ge(s_x[t], 16)
                if t > 0:
                    act.wait_ge(s_ssq, t)
                act.activation(squares[:, :], x_nat[:, t, :], ACT.Square, accum_out=x_ssq[:, t:t + 1]).then_inc(s_ssq, 1)

            x_square(0)
            round_unit(0, 0, first=True, pieces=(0,))
            turned_hi(0, 0, banks=(0,))
            round_unit(0, 0, first=True, pieces=(1,))
            act.dma_start(cs[:, :, :, :], rope_cs).then_inc(s_consts, 16)
            for n, w in enumerate((q_norm_w, k_norm_w)):
                act.dma_start(qk_w[:, n, :], w[0, :].partition_broadcast(P)).then_inc(s_consts, 16)
            for n, w in enumerate((lambda_q1, lambda_k1, lambda_q2, lambda_k2)):
                act.dma_start(lam_in[:, n, :], w[0, :].partition_broadcast(P)).then_inc(s_consts, 16)
            turned_hi(0, 0, banks=(1, 2, 3))
            round_unit(0, 1, first=True)
            x_square(1)
            x_square(2)
            turned_hi(0, 1)
            x_square(3)
            turned_hi(0, 2)
            turned_hi(0, 3)

            def act_block(blk, units=4):
                for m in range(units):
                    round_unit(blk * 2 + 1 + m // 2, m % 2)

            act_block(0)
            act.wait_ge(s_lam, 2)
            act.activation(lam_exp[:, :], lam_sum[:, :], ACT.Exp).then_inc(s_lam_exp, 1)
            with act.Fori(1, QKV_BLOCKS - 1) as blk:
                act_block(blk)

            def scores_exp(head, i):
                e = i % 2
                act.wait_ge(s_neg, head * 4 + i + 1)
                for c in range(2):
                    act.activation(expo[:, e, c, 0:(i + 1) * P], bank[:, SCORE_BANK[e] + c, 0:(i + 1) * P], ACT.Exp,
                                   bias=neg_peak[:, e, c:c + 1], scale=SCALE,
                                   accum_out=total[:, e, c:c + 1]).then_inc(s_exp, 1)

            def qk_out(head, part, b):
                act.wait_ge(s_qk_turn, head * 2 + part + 1)
                for c in range(2):
                    act.activation((q_t, k_t)[part][half_rows(c), c, :], bank[half_rows(c), b, :],
                                   ACT.Copy).then_inc(s_qk_t, 1)
                if part == 1:
                    for c in range(2):
                        act.wait_ge(s_qk_t, head * 6 + 3 + c)
                        act.activation(k_t[half_rows(1 - c), c, :], k_t[half_rows(c), c, :].bitcast(F32),
                                       ACT.Copy).then_inc(s_qk_t, 1)

            def qk_in(head, part):
                act.activation(rot[part][:, :, :], qkv[:, :, bass.ds(head * DV + part * HEADS * DV, DV)],
                               ACT.Copy).then_inc(s_qk_in, 1)

            def act_head(pair, sub, last=False):
                head = pair * 2 + sub
                for s in range(SLOTS):
                    if s - 2 in VALUES_AT:
                        i = VALUES_AT[s - 2]
                        act.wait_ge(s_orstd, head * 4 + i + 1)
                        act.activation(attn_n[:, :], bank[:, VALUE_BANK, 0:DV], ACT.Copy,
                                       scale=o_rstd[:, i % 2:i % 2 + 1]).then_inc(s_attn_n, 1)
                    if s - 1 in QK_TURN_AT and not last:
                        which = QK_TURN_AT[s - 1]
                        qk_out(head + 1, which, QK_BANKS[which])
                    if s in TURN_AT:
                        i = TURN_AT[s]
                        act.wait_ge(s_pturn, head * 4 + i + 1)
                        act.activation(probs_t[:, 0:(i + 1) * P], bank[:, TURN_BANK, 0:(i + 1) * P], ACT.Copy)\
                            .then_inc(s_probs_t, 1)
                    if s == 9:
                        act.wait_ge(s_used, head * 3 + U_HEAD + 1)
                        act.activation(gated[:, CONV_K - 1:CONV_K - 1 + SEQ], bank[:, sub, :], ACT.Copy).then_inc(s_act_out, 1)
                    if s - 2 in SCORES_AT:
                        scores_exp(head, SCORES_AT[s - 2])
                    if s - 1 in VALUES_AT:
                        i = VALUES_AT[s - 1]
                        act.wait_ge(s_values, head * 4 + i + 1)
                        act.activation(attn_n[:, :], bank[:, VALUE_BANK, 0:DV], ACT.Square,
                                       accum_out=o_ssq[:, i % 2:i % 2 + 1]).then_inc(s_ossq, 1)
                        act.wait_ge(s_ossq, head * 8 + 2 * i + 1)
                        act.activation(o_ms[:, i % 2:i % 2 + 1], o_ssq[:, i % 2:i % 2 + 1], ACT.Copy,
                                       bias=SUBLN_EPS, scale=1.0 / DV).then_inc(s_ossq, 1)
                    for n, at_slot in enumerate(ROUND_AT):
                        if s in (at_slot, at_slot + 1):
                            m = 3 * sub + 1 + n
                            round_unit(pair * 3 + U_HEAD // 2 + m // 2, m % 2, pieces=(s - at_slot,))
                    if s in (1, 2) and not last:
                        qk_in(head + 1, s - 1)

            act.wait_ge(s_emptied, E_QKV + ST * 3)
            qk_in(0, 0)
            qk_in(0, 1)
            act_block(QKV_BLOCKS - 1, units=3)
            qk_out(0, 0, TURN_BANK)
            qk_out(0, 1, VALUE_BANK)

            with act.Fori(0, HEADS // 2 - 1) as pair:
                act_head(pair, 0)
                act_head(pair, 1)
            act_head(HEADS // 2 - 1, 0)
            act_head(HEADS // 2 - 1, 1, last=True)

            act.activation(silu_g[:, 0:1], half_power[:, 0:1], ACT.Silu).then_inc(s_silu, 1)
            act.wait_ge(s_used, U_OUT)
            act.wait_ge(s_placed, 4 * HEADS)
            for g in range(4):
                if g == 1:
                    round_unit(U_OUT // 2, 1)
                elif g == 3:
                    act.wait_ge(s_emptied, E_OUT)
                for t in range(ST):
                    tile = (slice(None), slice(4 * g, 4 * g + 4), slice(t * P, (t + 1) * P))
                    act.activation(act_hi[tile], mixed[tile], ACT.Copy).then_inc(s_mix_hi, 1)
            act.dma_start(norm_w[:, :], ffn_norm_w[0, :].partition_broadcast(P)).then_inc(s_norm_w2, 16)
            act.wait_ge(s_low, KT)
            act.dma_start(resid[:, :, :], x_v).then_inc(s_resid, 16)

            def resid_square(blk, t):
                act.wait_ge(s_emptied, blk * ST + E_OUT + t + 1)
                act.wait_ge(s_ssq, blk * ST + ST + t)
                act.activation(squares[:, 0:NB], resid[:, t, bass.ds(blk * NB, NB)], ACT.Square,
                               accum_out=r_part[:, t, bass.ds(blk, 1)]).then_inc(s_ssq, 1)

            with act.Fori(0, OUT_BLOCKS - 1) as blk:
                for m in range(4):
                    round_unit(blk * 2 + U_OUT // 2 + 1 + m // 2, m % 2)
                for t in range(ST):
                    resid_square(blk, t)
            for m in range(3):
                round_unit(U_FF // 2 - 1 + m // 2, m % 2)
            for t in range(ST):
                resid_square(OUT_BLOCKS - 1, t)
                if t == 2:
                    turned_hi(1, 0)
            turned_hi(1, 1)
            round_unit(U_FF // 2, 1)
            turned_hi(1, 2)
            turned_hi(1, 3)

            def act_gate_up(c, j):
                unit = c * (U_CHUNK // 2) + j + U_FF // 2
                round_unit(unit + 1, 0)
                act.activation(silu_g[:, :], bank[:, 0, :], ACT.Silu).then_inc(s_act_out, 1)
                round_unit(unit + 1, 1)
                act.wait_ge(s_emptied, c * E_CHUNK + j + E_FF + 1)
                act.activation(hid_hi[:, bass.ds(j, 1), :].rearrange("p a s -> p (a s)"), hidden[:, :], ACT.Copy).then_inc(s_hid_hi, 1)

            def act_down(c, d, last=False):
                for m in range(6):
                    if last and m >= 4:
                        continue
                    size = DOWN_UNITS[2] * NB if m % 3 == 0 else UNIT
                    round_unit(c * (U_CHUNK // 2) + d * 3 + U_FF // 2 + CF + 1 + m // 2, m % 2, size)

            def act_chunk(c, last=False):
                with act.Fori(0, CF) as j:
                    act_gate_up(c, j)
                if last:
                    for d in range(OUT_BLOCKS // 2):
                        act_down(c, d, last=d == OUT_BLOCKS // 2 - 1)
                else:
                    with act.Fori(0, OUT_BLOCKS // 2) as d:
                        act_down(c, d)

            act.wait_ge(s_silu, 1)
            with act.Fori(0, CHUNKS - 1) as c:
                act_chunk(c)
            act_chunk(CHUNKS - 1, last=True)

        @block.vector
        def _(dve):
            def low_unit(half, parity, size=UNIT, pieces=(0, 1)):
                for q in pieces:
                    dve.wait_ge(s_whi, half * 4 + 2 * parity + q + 1)
                    part = slice(q * size // 2, (q + 1) * size // 2)
                    dve.tensor_tensor(w_lo[:, parity, part], w_raw[:, parity, part],
                                      w_hi[:, parity, part].bitcast(F32), ALU.subtract).then_inc(s_wlo, 1)

            def scale_rows(phase, t):
                g = ST * phase + t
                dve.wait_ge(s_rstd, 2 * g + 2)
                if t >= 2:
                    dve.wait_ge(s_turned, 4 * (g - 1))
                dve.scalar_tensor_tensor(out=scaled[:, t % 2, :], in0=(x_nat, resid)[phase][:, t, :],
                                         scalar=x_rstd[:, phase, t:t + 1], in1=norm_w[:, :],
                                         op0=ALU.mult, op1=ALU.mult).then_inc(s_scaled, 1)

            def turned_lo(phase, t, banks=range(4)):
                for b in banks:
                    dve.wait_ge(s_act_hi, 4 * (ST * phase + t) + b + 1)
                    src = bank[:, NORM_BANK[phase][t] + b, :].rearrange("p (k s) -> p k s", s=P)
                    tile = (slice(None), slice(4 * b, 4 * b + 4), slice(t * P, (t + 1) * P))
                    dve.tensor_tensor(act_lo[tile], src, act_hi[tile].bitcast(F32), ALU.subtract).then_inc(s_emptied, 1)

            dve.memset(gated[:, 0:CONV_K - 1], 0.0).then_inc(s_pad, 1)
            for c in range(2):
                dve.memset(k_t_lo[half_rows(1 - c), c, :].bitcast(F32), 0.0).then_inc(s_pad, 1)
            dve.wait_ge(s_norm_w, 16)
            for t in range(ST):
                scale_rows(0, t)
                if t > 0:
                    turned_lo(0, t)
                else:
                    low_unit(0, 0, pieces=(0,))
                    turned_lo(0, 0, banks=(0,))
                    low_unit(0, 0, pieces=(1,))
                    turned_lo(0, 0, banks=(1, 2, 3))
                    low_unit(0, 1)
                    dve.wait_ge(s_rows_t, 1)
                    dve.tensor_copy(taps[:, :], bank[:, TAPS_BANK, 0:CONV_K * HEADS + 1]).then_inc(s_taps, 1)
            dve.wait_ge(s_consts, 16 * CONSTS)
            dve.tensor_tensor(lam_in[:, 0:4:2, :], lam_in[:, 0:4:2, :], lam_in[:, 1:4:2, :], ALU.mult).then_inc(s_lam, 1)
            dve.wait_ge(s_lam, 1)
            dve.tensor_reduce(lam_sum[:, :], lam_in[:, 0:4:2, :], AX.X, ALU.add).then_inc(s_lam, 1)

            def prep_mean_square(head, part):
                dve.wait_ge(s_prep, head * (2 * PREP) + part * PREP + 2)
                dve.tensor_reduce(qk_ssq[:, :], rot_tmp[:, :, :].rearrange("p t (c e) -> p (t c) e", c=2),
                                  AX.X, ALU.add).then_inc(s_prep_ms, 1)
                dve.wait_ge(s_prep_ms, head * 4 + 2 * part + 1)
                dve.tensor_scalar(qk_ms[:, :], qk_ssq[:, :], 1.0 / DK, EPS, ALU.mult, ALU.add).then_inc(s_prep_ms, 1)

            def qk_low(head, part, b):
                dve.wait_ge(s_qk_t, head * 6 + 2 * part + 2)
                for c in range(2):
                    out_ = q_t[half_rows(1 - c), c, :] if part == 0 else k_t_lo[half_rows(c), c, :]
                    dve.tensor_tensor(out_, bank[half_rows(c), b, :], (q_t, k_t)[part][half_rows(c), c, :].bitcast(F32),
                                      ALU.subtract).then_inc(s_qk_lo, 1)

            last_blk = QKV_BLOCKS - 1

            def dve_block(blk, units=4):
                for m in range(units):
                    if blk is last_blk and m < 2:
                        prep_mean_square(0, m)
                    low_unit(blk * 2 + 1 + m // 2, m % 2)
                    if m == 2:
                        if blk is last_blk:
                            qk_low(0, 0, TURN_BANK)
                            qk_low(0, 1, VALUE_BANK)
                        for t in range(ST):
                            if t < ST - 1:
                                dve.wait_ge(s_tile, blk * (ST - 1) + t + 1)
                            else:
                                dve.wait_ge(s_used, blk * 4 + 4)
                            dve.tensor_copy(qkv[:, t, bass.ds(blk * NB, NB)], bank[:, t, :]).then_inc(s_emptied, 1)

            dve_block(0)
            dve.wait_ge(s_lam_exp, 1)
            dve.tensor_scalar(neg_lam[:, 0:1], lam_exp[:, 1:2], -LAMBDA_INIT, None, ALU.add).then_inc(s_lam, 1)
            dve.wait_ge(s_lam, 3)
            dve.tensor_tensor(neg_lam[:, 1:2], neg_lam[:, 0:1], lam_exp[:, 0:1], ALU.subtract).then_inc(s_lam, 1)
            dve.wait_ge(s_lam, 4)
            with dve.Fori(1, last_blk) as blk:
                dve_block(blk)
            dve_block(last_blk, units=3)
            dve.wait_ge(s_pad, 3)

            def softmax_peak(head, i):
                e, n = i % 2, (i + 1) * P
                banks = slice(SCORE_BANK[e], SCORE_BANK[e] + 2)
                dve.wait_ge(s_scores, head * 4 + i + 1)
                dve.memset(bank[0:CHUNK, banks, n - CHUNK:n], MASKED).then_inc(s_mask, 1)
                dve.wait_ge(s_mask, head * 4 + i + 1)
                dve.tensor_reduce(peak[:, e, :], bank[:, banks, 0:n], AX.X, ALU.max).then_inc(s_peak, 1)
                dve.wait_ge(s_peak, head * 4 + i + 1)
                dve.tensor_scalar(neg_peak[:, e, :], peak[:, e, :], -SCALE, None, ALU.mult).then_inc(s_neg, 1)

            def softmax_combine(head, i):
                e, n = i % 2, (i + 1) * P
                dve.wait_ge(s_exp, head * 8 + 2 * i + 2)
                dve.reciprocal(share[:, e, :], total[:, e, :]).then_inc(s_share, 1)
                dve.wait_ge(s_share, head * 12 + 3 * i + 1)
                dve.tensor_scalar(expo[:, e, 0, 0:n], expo[:, e, 0, 0:n], share[:, e, 0:1], None, ALU.mult).then_inc(s_share, 1)
                dve.tensor_tensor(share[:, e, 1:2], share[:, e, 1:2], neg_lam[:, 1:2], ALU.mult).then_inc(s_share, 1)
                dve.wait_ge(s_share, head * 12 + 3 * i + 3)
                dve.scalar_tensor_tensor(out=expo[:, e, 0, 0:n], in0=expo[:, e, 1, 0:n], scalar=share[:, e, 1:2],
                                         in1=expo[:, e, 0, 0:n], op0=ALU.mult, op1=ALU.add).then_inc(s_probs, 1)

            def dve_head(pair, sub, last=False):
                head = pair * 2 + sub
                conv_out = mixed[:, bass.ds(head + HEADS, 1), :].rearrange("p a s -> p (a s)")

                def tap(j):
                    return taps[:, bass.ds(head + j * HEADS, 1)]

                for s in range(SLOTS):
                    if s - 1 in SCORES_AT:
                        softmax_peak(head, SCORES_AT[s - 1])
                    if s - 3 in SCORES_AT:
                        softmax_combine(head, SCORES_AT[s - 3])
                    if s == 16:
                        dve.wait_ge(s_act_out, head + 1)
                        dve.wait_ge(s_used, head * 3 + U_HEAD + 2)
                        u = gated[:, CONV_K - 1:CONV_K - 1 + SEQ]
                        dve.tensor_tensor(u, u, bank[:, 1 - sub, :], ALU.mult).then_inc(s_emptied, 1)
                    if s - 1 in PLACE_AT:
                        i = PLACE_AT[s - 1]
                        dve.wait_ge(s_oturn, head * 4 + i + 1)
                        dve.tensor_scalar(mixed[:, bass.ds(head, 1), i * P:(i + 1) * P].rearrange("p a s -> p (a s)"),
                                          bank[:, VALUE_BANK, 0:P], taps[:, CONV_K * HEADS:CONV_K * HEADS + 1],
                                          1.0 - LAMBDA_INIT, ALU.mult, ALU.mult).then_inc(s_placed, 1)
                    if s - 1 in QK_TURN_AT and not last:
                        which = QK_TURN_AT[s - 1]
                        qk_low(head + 1, which, QK_BANKS[which])
                    if s in (2, 10) and not last:
                        prep_mean_square(head + 1, s // 8)
                    for n, at_slot in enumerate(ROUND_AT):
                        if s in (at_slot + 1, at_slot + 3):
                            m = 3 * sub + 1 + n
                            low_unit(pair * 3 + U_HEAD // 2 + m // 2, m % 2, pieces=((s - at_slot) // 2,))
                    if s in (18, 19, 21):
                        j = (18, 19, 21).index(s)
                        shift = gated[:, CONV_K - 1 - j:CONV_K - 1 - j + SEQ]
                        if j == 0:
                            dve.wait_ge(s_emptied, head * 2 + E_HEAD + 1)
                            dve.tensor_scalar(conv_out, shift, tap(CONV_K - 1), None, ALU.mult).then_inc(s_conv, 1)
                        else:
                            dve.wait_ge(s_conv, head * CONV_K + j)
                            dve.scalar_tensor_tensor(out=conv_out, in0=shift, scalar=tap(CONV_K - 1 - j), in1=conv_out,
                                                     op0=ALU.mult, op1=ALU.add).then_inc(s_conv, 1)
                dve.wait_ge(s_conv, head * CONV_K + CONV_K)
                dve.wait_ge(s_used, head * 3 + U_HEAD + 3)
                dve.tensor_tensor(conv_out, bank[:, sub, :], conv_out, ALU.mult).then_inc(s_emptied, 1)

            with dve.Fori(0, HEADS // 2 - 1) as pair:
                dve_head(pair, 0)
                dve_head(pair, 1)
            dve_head(HEADS // 2 - 1, 0)
            dve_head(HEADS // 2 - 1, 1, last=True)

            for g in range(4):
                if g == 1:
                    low_unit(U_OUT // 2, 1)
                for t in range(ST):
                    dve.wait_ge(s_mix_hi, 4 * g + t + 1)
                    tile = (slice(None), slice(4 * g, 4 * g + 4), slice(t * P, (t + 1) * P))
                    dve.tensor_tensor(act_lo[tile], mixed[tile], act_hi[tile].bitcast(F32), ALU.subtract).then_inc(s_low, 1)

            def add_tile(columns, b, t):
                dve.tensor_tensor(resid[:, t, columns], bank[:, b, :], resid[:, t, columns], ALU.add).then_inc(s_emptied, 1)

            def resid_ssq(t):
                dve.wait_ge(s_ssq, ST + ST * (OUT_BLOCKS - 1) + t + 1)
                dve.tensor_reduce(r_ssq[:, t:t + 1], r_part[:, t, :], AX.X, ALU.add).then_inc(s_rsum, 1)

            def out_tile(blk, t):
                if t < ST - 1:
                    dve.wait_ge(s_tile, blk * (ST - 1) + T_OUT + t + 1)
                else:
                    dve.wait_ge(s_used, blk * 4 + U_OUT + 4)
                add_tile(bass.ds(blk * NB, NB), t, t)

            def dve_out_block(blk, first=False):
                for m in range(4):
                    if m == 3:
                        if first:
                            dve.wait_ge(s_resid, 16)
                        for t in range(ST):
                            out_tile(blk, t)
                    low_unit(blk * 2 + U_OUT // 2 + 1 + m // 2, m % 2)

            dve_out_block(0, first=True)
            with dve.Fori(1, OUT_BLOCKS - 1) as blk:
                dve_out_block(blk)
            low_unit(U_FF // 2 - 1, 0)
            low_unit(U_FF // 2 - 1, 1)
            last = OUT_BLOCKS - 1
            out_tile(last, 0)
            low_unit(U_FF // 2, 0, pieces=(0,))
            resid_ssq(0)
            low_unit(U_FF // 2, 0, pieces=(1,))
            dve.wait_ge(s_norm_w2, 16)
            scale_rows(1, 0)
            out_tile(last, 1)
            out_tile(last, 2)
            resid_ssq(1)
            scale_rows(1, 1)
            out_tile(last, 3)
            turned_lo(1, 0)
            resid_ssq(2)
            resid_ssq(3)
            turned_lo(1, 1)
            low_unit(U_FF // 2, 1)
            scale_rows(1, 2)
            scale_rows(1, 3)
            turned_lo(1, 2)
            turned_lo(1, 3)

            def dve_gate_up(c, j):
                unit = c * (U_CHUNK // 2) + j + U_FF // 2
                low_unit(unit + 1, 0)
                dve.wait_ge(s_act_out, c * CF + j + HEADS + 1)
                dve.wait_ge(s_used, unit * 2 + 2)
                dve.wait_ge(s_low, c * CF + KT + j)
                dve.tensor_tensor(hidden[:, :], bank[:, 1, :], silu_g[:, :], ALU.mult).then_inc(s_emptied, 1)
                low_unit(unit + 1, 1)
                dve.wait_ge(s_hid_hi, c * CF + j + 1)
                dve.tensor_tensor(hid_lo[:, bass.ds(j, 1), :].rearrange("p a s -> p (a s)"), hidden[:, :],
                                  hid_hi[:, bass.ds(j, 1), :].rearrange("p a s -> p (a s)").bitcast(F32),
                                  ALU.subtract).then_inc(s_low, 1)

            def dve_down(c, d, last=False):
                for m in range(6):
                    sub, part = divmod(m, 3)
                    unit = c * (U_CHUNK // 2) + d * 3 + U_FF // 2 + CF + m // 2
                    if part == 2:
                        for t in range(ST):
                            if t < ST - 1:
                                dve.wait_ge(s_tile, c * T_CHUNK + d * (2 * (ST - 1)) + T_FF + (ST - 1) * sub + t + 1)
                            else:
                                dve.wait_ge(s_used, unit * 2 + m % 2 + 1)
                            add_tile(bass.ds(d * (2 * NB) + sub * NB, NB), DOWN_BANKS[sub][t], t)
                    if not (last and m >= 4):
                        low_unit(unit + 1, m % 2, DOWN_UNITS[2] * NB if part == 0 else UNIT)

            def dve_chunk(c, last=False):
                with dve.Fori(0, CF) as j:
                    dve_gate_up(c, j)
                if last:
                    for d in range(OUT_BLOCKS // 2):
                        dve_down(c, d, last=d == OUT_BLOCKS // 2 - 1)
                else:
                    with dve.Fori(0, OUT_BLOCKS // 2) as d:
                        dve_down(c, d)

            with dve.Fori(0, CHUNKS - 1) as c:
                dve_chunk(c)
            dve_chunk(CHUNKS - 1, last=True)

        @block.tensor
        def _(pe):
            def product(dst, left, right, start, stop):
                pe.matmul(dst, left[0], right[0], start=start, stop=False)
                pe.matmul(dst, left[0], right[1], start=False, stop=False)
                return pe.matmul(dst, left[1], right[0], start=False, stop=stop)

            def turn_rows(phase, t):
                g = ST * phase + t
                pe.wait_ge(s_scaled, g + 1)
                for b in range(4):
                    if phase == 1:
                        pe.wait_ge(s_emptied, E_NORM2 + 4 * (t - 1 - (t == 1)) + b + 1 if t else E_NORM2 - ST)
                    elif t > 0:
                        pe.wait_ge(s_emptied, 4 * (t - 1) + b + 1)
                    for k in range(4):
                        ins = pe.transpose(bank[:, NORM_BANK[phase][t] + b, k * P:(k + 1) * P],
                                           scaled[:, t % 2, (4 * b + k) * P:(4 * b + k + 1) * P], ident[:, :])
                    ins.then_inc(s_turned, 1)

            def block_tile(half, m, t, free=None, operand=None):
                if m == 0 and free is not None:
                    pe.wait_ge(s_emptied, free)
                if operand is not None:
                    pe.wait_ge(*operand)
                for k in range(UK):
                    if t == 0 and k in (0, UK // 2):
                        pe.wait_ge(s_wlo, half * 4 + 2 * (m % 2) + 1 + k // (UK // 2))
                    ins = product(bank[:, t, :],
                                  tuple(a[:, UK * m + k, t * P:(t + 1) * P] for a in (act_hi, act_lo)),
                                  (moving(w_hi, m % 2)[:, k, :], moving(w_lo, m % 2)[:, k, :]),
                                  m == 0 and k == 0, m == 3 and k == UK - 1)
                if t == ST - 1:
                    ins.then_inc(s_used, 1)
                elif m == 3:
                    ins.then_inc(s_tile, 1)

            pe.wait_ge(s_ident, 2)
            with pe.Fori(0, WARM_STEPS):
                for k in range(4):
                    pe.transpose(bank[:, VALUE_BANK, k * P:(k + 1) * P], ident[:, :], ident[:, :])
            pe.wait_ge(s_rows, 32)
            pe.transpose(bank[:, TAPS_BANK, 0:CONV_K * HEADS + 1], rows[0:CONV_K * HEADS + 1, :],
                         ident[0:CONV_K * HEADS + 1, 0:CONV_K * HEADS + 1]).then_inc(s_rows_t, 1)
            for t in range(ST):
                if t < 2:
                    turn_rows(0, t)
                if t == TAPS_BANK:
                    pe.wait_ge(s_taps, 1)
                for m in range(2):
                    block_tile(0, m, t, operand=(s_emptied, 4 * t + m + 1))
                    if m == 0 and 1 <= t < ST - 1:
                        turn_rows(0, t + 1)
            for m in range(2, 4):
                for t in range(ST):
                    block_tile(1, m, t, operand=(s_emptied, 4 * t + m + 1))

            with pe.Fori(1, QKV_BLOCKS - 1) as blk:
                for m in range(4):
                    for t in range(ST):
                        block_tile(blk * 2 + m // 2, m, t, free=blk * ST + E_QKV - ST + t + 1)

            def qk_turn(head, part, b):
                pe.wait_ge(s_prep, head * (2 * PREP) + (part + 1) * PREP + 1)
                for t in range(ST):
                    ins = pe.transpose(bank[:, b, t * P:(t + 1) * P], rot[part][:, t, :], ident[:, :])
                ins.then_inc(s_qk_turn, 1)

            def scores(head, i):
                if i == 0:
                    pe.wait_ge(s_qk_t, head * 6 + 6)
                    pe.wait_ge(s_qk_lo, head * 4 + 4)
                if i == 1:
                    pe.wait_ge(s_emptied, E_HEAD)
                if i >= 2:
                    pe.wait_ge(s_exp, head * 8 + 2 * (i - 2) + 2)
                for c in range(2):
                    dst, q = bank[:, SCORE_BANK[i % 2] + c, 0:(i + 1) * P], q_t[:, c, i * P:(i + 1) * P]
                    pe.matmul(dst, q, k_t[:, c, 0:(i + 1) * P], start=True, stop=False)
                    ins = pe.matmul(dst, q, k_t_lo[:, c, 0:(i + 1) * P], start=False, stop=True)
                ins.then_inc(s_scores, 1)

            def turn_probs(head, i):
                pe.wait_ge(s_probs, head * 4 + i + 1)
                for b in range(i + 1):
                    ins = pe.transpose(bank[:, TURN_BANK, b * P:(b + 1) * P], expo[:, i % 2, 0, b * P:(b + 1) * P], ident[:, :])
                ins.then_inc(s_pturn, 1)

            def values(head, i):
                pe.wait_ge(s_probs_t, head * 4 + i + 1)
                if i > 0:
                    pe.wait_ge(s_placed, head * 4 + i)
                for b in range(i + 1):
                    ins = pe.matmul(bank[:, VALUE_BANK, 0:DV], probs_t[:, b * P:(b + 1) * P],
                                    qkv[:, b, bass.ds(head * DV + 2 * HEADS * DV, DV)], start=b == 0, stop=b == i)
                ins.then_inc(s_values, 1)

            def turn_attn(head, i):
                pe.wait_ge(s_attn_n, head * 4 + i + 1)
                pe.transpose(bank[:, VALUE_BANK, 0:P], attn_n[:, :], ident[:, :]).then_inc(s_oturn, 1)

            def pe_head(pair, sub, last=False):
                head = pair * 2 + sub
                conv_bank = (sub, 1 - sub, sub)
                for s in range(SLOTS):
                    part = s // 8
                    m = 3 * sub + part
                    if s % 8 == 0:
                        pe.wait_ge(s_wlo, pair * 12 + 2 * U_HEAD + 2 * m + 1)
                        if part < 2:
                            pe.wait_ge(s_emptied, head * 2 + E_HEAD - 1 + part)
                        else:
                            pe.wait_ge(s_act_out, head + 1)
                    elif s % 8 == 4:
                        pe.wait_ge(s_wlo, pair * 12 + 2 * U_HEAD + 2 * m + 2)
                    if s in SCORES_AT:
                        scores(head, SCORES_AT[s])
                    if s in TURN_AT:
                        turn_probs(head, TURN_AT[s])
                    if s in VALUES_AT:
                        values(head, VALUES_AT[s])
                    if s in PLACE_AT:
                        turn_attn(head, PLACE_AT[s])
                    if s in QK_TURN_AT and not last:
                        which = QK_TURN_AT[s]
                        qk_turn(head + 1, which, QK_BANKS[which])
                    for k in range(2 * (s % 8), 2 * (s % 8) + 2):
                        ins = product(bank[:, conv_bank[part], :],
                                      (stationary(w_hi, m % 2)[:, k, :], stationary(w_lo, m % 2)[:, k, :]),
                                      (act_hi[:, k, :], act_lo[:, k, :]), k == 0, k == KT - 1)
                    if s % 8 == 7:
                        ins.then_inc(s_used, 1)

            last_blk = QKV_BLOCKS - 1
            for m in range(4):
                if m == 3:
                    pe.wait_ge(s_emptied, E_QKV + ST * last_blk)
                    for part in range(2):
                        qk_turn(0, part, (TURN_BANK, VALUE_BANK)[part])
                for t in range(ST):
                    block_tile(last_blk * 2 + m // 2, m, t, free=E_QKV + ST * (last_blk - 1) + t + 1)

            with pe.Fori(0, HEADS // 2 - 1) as pair:
                pe_head(pair, 0)
                pe_head(pair, 1)
            pe_head(HEADS // 2 - 1, 0)
            pe_head(HEADS // 2 - 1, 1, last=True)

            def out_unit_tile(blk, m, t):
                block_tile(blk * 2 + U_OUT // 2 + m // 2, m, t, free=blk * ST + E_OUT - ST + t + 1,
                           operand=(s_low, 4 * m + t + 1))

            pe.wait_ge(s_emptied, E_OUT)
            with pe.Fori(0, OUT_BLOCKS - 1) as blk:
                for m in range(4):
                    for t in range(ST):
                        out_unit_tile(blk, m, t)
            for m in range(4):
                for t in range(ST):
                    if m == 3 and t == ST - 1:
                        turn_rows(1, 0)
                    out_unit_tile(OUT_BLOCKS - 1, m, t)
            turn_rows(1, 1)

            def hidden_columns(parity, columns, turned=None):
                for k in range(KT):
                    if turned is not None and k % 4 == 0:
                        pe.wait_ge(s_emptied, turned + k // 4 + 1)
                    ins = product(bank[:, parity, columns],
                                  (stationary(w_hi, parity)[:, k, :], stationary(w_lo, parity)[:, k, :]),
                                  (act_hi[:, k, columns], act_lo[:, k, columns]), k == 0, k == KT - 1)
                return ins

            for h in range(2):
                if h == 1:
                    turn_rows(1, 3)
                for parity in range(2):
                    if h == 0:
                        pe.wait_ge(s_wlo, 2 * U_FF + 2 * parity + 2)
                    ins = hidden_columns(parity, slice(h * 2 * P, (h + 1) * 2 * P),
                                         turned=E_NORM2 + 8 * h + 4 if parity == 0 else None)
                    if h == 1:
                        ins.then_inc(s_used, 1)
                    elif parity == 0:
                        turn_rows(1, 2)

            def pe_gate_up(c, j):
                unit = c * (U_CHUNK // 2) + j + U_FF // 2
                for parity in range(2):
                    pe.wait_ge(s_wlo, unit * 4 + 2 * parity + 2)
                    if parity == 0:
                        pe.wait_ge(s_act_out, c * CF + j + HEADS)
                        pe.wait_ge(s_emptied, c * E_CHUNK + j + E_FF - ST)
                    else:
                        pe.wait_ge(s_emptied, c * E_CHUNK + j + E_FF)
                    hidden_columns(parity, slice(0, SEQ)).then_inc(s_used, 1)

            def pe_down(c, d):
                for m in range(6):
                    sub, part = divmod(m, 3)
                    first = UK * part
                    pe.wait_ge(s_low, c * CF + KT + first + DOWN_UNITS[part])
                    down_unit(c, d, m, sub, part, first)

            def down_unit(c, d, m, sub, part, first):
                half = c * (U_CHUNK // 2) + d * 3 + U_FF // 2 + CF + m // 2
                pe.wait_ge(s_wlo, half * 4 + 2 * (m % 2) + 2)
                for t in range(ST):
                    if part == 0:
                        pe.wait_ge(s_emptied, c * E_CHUNK + d * (2 * ST) + E_FF + CF + ST * (sub - 2) + (t + 1 if t < 2 or sub else ST + ST))
                    for k in range(DOWN_UNITS[part]):
                        ins = product(bank[:, DOWN_BANKS[sub][t], :],
                                      tuple(a[:, first + k, t * P:(t + 1) * P] for a in (hid_hi, hid_lo)),
                                      (moving(w_hi, m % 2)[:, k, :], moving(w_lo, m % 2)[:, k, :]),
                                      part == 0 and k == 0, part == 2 and k == DOWN_UNITS[part] - 1)
                    if part == 2 and t < ST - 1:
                        ins.then_inc(s_tile, 1)
                ins.then_inc(s_used, 1)

            with pe.Fori(1, CF) as j:
                pe_gate_up(0, j)
            with pe.Fori(0, OUT_BLOCKS // 2) as d:
                pe_down(0, d)
            with pe.Fori(1, CHUNKS) as c:
                with pe.Fori(0, CF) as j:
                    pe_gate_up(c, j)
                with pe.Fori(0, OUT_BLOCKS // 2) as d:
                    pe_down(c, d)


_INS = ["x", "attn_norm_w", "w_in", "q_norm_w", "k_norm_w", "lambda_q1", "lambda_k1", "lambda_q2", "lambda_k2",
        "subln_w", "conv_w", "w_out", "ffn_norm_w", "w_gate", "w_up", "w_down"]


def kernel(**inputs):
    import numpy as _np
    import concourse.bacc as _bacc
    from concourse import mybir as _mybir
    from concourse.bass_utils import run_bass_kernel_spmd as _run

    nc = _bacc.Bacc("TRN2", target_bir_lowering=False, num_devices=1, dynamic_dma_scratch_size=1024)
    arrays, args = {}, []
    for name in _INS:
        a = _np.ascontiguousarray(inputs[name])
        arrays[f"in_{name}_dram"] = a
        args.append(nc.dram_tensor(f"in_{name}_dram", a.shape, _mybir.dt.from_np(a.dtype), kind="ExternalInput").ap())
    tables = rope_tables()
    arrays["rope_dram"] = tables
    args.append(nc.dram_tensor("rope_dram", tables.shape, F32, kind="ExternalInput").ap())
    args.append(nc.dram_tensor("out_dram", (1, SEQ, D), F32, kind="ExternalOutput").ap())
    build(nc, *args)
    r = _run(nc, [arrays], core_ids=[0])
    return r.results[0]["out_dram"]
```
